# Optimizing a Trainium2 kernel written in Bass

```python
import jax, jax.numpy as jnp
from jax import lax
import numpy as np

D_MODEL = 2048
BATCH = 1
SEQ = 256
DEPTH = 2

N_MIXERS = 2
HGRN_EXPAND = 128
HGRN_HEADS = D_MODEL // HGRN_EXPAND
HGRN_F_DIM = HGRN_HEADS * HGRN_EXPAND
HGRN_I_DIM = D_MODEL
HGRN_HEAD_I = HGRN_I_DIM // HGRN_HEADS
CHUNK = 64
CONV_WIDTH = 3
D_FF = 5632
EPS = 1e-6
N_HGRN = (DEPTH + 1) // 2
N_SC = DEPTH // 2

kernel_name = "hgrn2_shortconv_interleaved_trunk"

def rms_norm(x, w):
    x32 = x.astype(jnp.float32)
    y = x32 * lax.rsqrt(jnp.mean(x32 * x32, axis=-1, keepdims=True) + EPS)
    return (y * w.astype(jnp.float32)).astype(x.dtype)

def causal_dwconv(u, w):
    K = w.shape[0]
    T = u.shape[1]
    up = jnp.pad(u, ((0, 0), (K - 1, 0), (0, 0)))
    return sum(up[:, k:k + T] * w[k] for k in range(K))

def chunked_gated_recurrence(q, k, v, logf):
    B, T, H, dk = q.shape
    dv = v.shape[-1]
    n = T // CHUNK

    def to_chunks(a):
        return a.reshape(B, n, CHUNK, H, a.shape[-1]).transpose(1, 0, 3, 2, 4)

    causal = jnp.tril(jnp.ones((CHUNK, CHUNK), dtype=bool))

    def step(S, inp):
        qc, kc, vc, gc = inp
        b = jnp.cumsum(gc, axis=2)
        rel = b[:, :, :, None, :] - b[:, :, None, :, :]
        rel = jnp.where(causal[:, :, None], rel, -jnp.inf)
        A = jnp.einsum('bhtd,bhsd,bhtsd->bhts', qc, kc, jnp.exp(rel))
        o = jnp.einsum('bhts,bhsv->bhtv', A, vc) + jnp.einsum('bhtd,bhdv->bhtv', qc * jnp.exp(b), S)
        b_last = b[:, :, -1:, :]
        S = jnp.exp(b_last[:, :, 0, :])[..., None] * S + jnp.einsum(
            'bhsd,bhsv->bhdv', kc * jnp.exp(b_last - b), vc)
        return S, o

    S0 = jnp.zeros((B, H, dk, dv), jnp.float32)
    _, o = lax.scan(step, S0, (to_chunks(q), to_chunks(k), to_chunks(v), to_chunks(logf)))
    return o.transpose(1, 0, 3, 2, 4).reshape(B, T, H * dv)

def hgrn2_mixer(xn, w_in, lb, out_gain, w_out):
    B, T, _ = xn.shape
    proj = xn @ w_in
    q, fr, v, g = jnp.split(proj, [HGRN_F_DIM, 2 * HGRN_F_DIM, 2 * HGRN_F_DIM + HGRN_I_DIM], axis=-1)
    q = jax.nn.silu(q.astype(jnp.float32)) * (HGRN_EXPAND ** -0.5)
    f = lb + (1.0 - lb) * jax.nn.sigmoid(fr.astype(jnp.float32))
    k = 1.0 - f
    logf = jnp.log(f)

    def heads(a, d):
        return a.reshape(B, T, HGRN_HEADS, d).astype(jnp.float32)

    o = chunked_gated_recurrence(heads(q, HGRN_EXPAND), heads(k, HGRN_EXPAND),
                                 heads(v, HGRN_HEAD_I), heads(logf, HGRN_EXPAND))
    o = rms_norm(o, out_gain) * jax.nn.silu(g.astype(jnp.float32))
    return (o @ w_out.astype(jnp.float32)).astype(xn.dtype)

def short_conv_mixer(xn, w_in, conv_w, w_out):
    proj = xn @ w_in
    gb, gc, h = jnp.split(proj, 3, axis=-1)
    y = gb * causal_dwconv(gc * h, conv_w)
    return y @ w_out

def conv_glu_ffn(xn, w_up, conv_w, w_down):
    u = causal_dwconv(xn @ w_up, conv_w)
    gate, val = jnp.split(u, 2, axis=-1)
    return (jax.nn.silu(gate) * val) @ w_down

def setup_inputs(seed: int = 0) -> dict:
    key = jax.random.key(seed)
    ks = jax.random.split(key, 16)
    f32 = jnp.float32

    def w(k, shape, fan_in):
        return jax.random.normal(k, shape, f32) * (fan_in ** -0.5)

    def gain(k, shape):
        return 1.0 + 0.02 * jax.random.normal(k, shape, f32)

    return {
        "x": jax.random.normal(ks[0], (BATCH, SEQ, D_MODEL), f32),
        "norm_mix": gain(ks[1], (DEPTH, D_MODEL)),
        "norm_ffn": gain(ks[2], (DEPTH, D_MODEL)),
        "hgrn_w_in": w(ks[3], (N_HGRN, D_MODEL, 2 * HGRN_F_DIM + 2 * HGRN_I_DIM), D_MODEL),
        "hgrn_lb_table": 0.1 * jax.random.normal(ks[4], (DEPTH + 1, HGRN_F_DIM), f32),
        "hgrn_out_norm": gain(ks[5], (N_HGRN, HGRN_I_DIM)),
        "hgrn_w_out": w(ks[6], (N_HGRN, HGRN_I_DIM, D_MODEL), HGRN_I_DIM),
        "sc_w_in": w(ks[7], (N_SC, D_MODEL, 3 * D_MODEL), D_MODEL),
        "sc_conv": w(ks[8], (N_SC, CONV_WIDTH, D_MODEL), CONV_WIDTH),
        "sc_w_out": w(ks[9], (N_SC, D_MODEL, D_MODEL), D_MODEL),
        "ffn_w_up": w(ks[10], (DEPTH, D_MODEL, 2 * D_FF), D_MODEL),
        "ffn_conv": w(ks[11], (DEPTH, CONV_WIDTH, 2 * D_FF), CONV_WIDTH),
        "ffn_w_down": w(ks[12], (DEPTH, D_FF, D_MODEL), D_FF),
        "final_norm": gain(ks[13], (D_MODEL,)),
    }

def reference(x, norm_mix, norm_ffn, hgrn_w_in, hgrn_lb_table, hgrn_out_norm, hgrn_w_out,
              sc_w_in, sc_conv, sc_w_out, ffn_w_up, ffn_conv, ffn_w_down, final_norm):
    lb_all = jnp.cumsum(jax.nn.softmax(hgrn_lb_table.astype(jnp.float32), axis=0), axis=0)
    h = x
    for i in range(DEPTH):
        j = i // N_MIXERS
        xn = rms_norm(h, norm_mix[i])
        if i % N_MIXERS == 0:
            mix = hgrn2_mixer(xn, hgrn_w_in[j], lb_all[i], hgrn_out_norm[j], hgrn_w_out[j])
        else:
            mix = short_conv_mixer(xn, sc_w_in[j], sc_conv[j], sc_w_out[j])
        h = h + mix.astype(h.dtype)
        h = h + conv_glu_ffn(rms_norm(h, norm_ffn[i]), ffn_w_up[i], ffn_conv[i], ffn_w_down[i]).astype(h.dtype)
    return rms_norm(h, final_norm)


_drawn_inputs = setup_inputs


def setup_inputs(seed=0):
    import zlib

    import numpy as np

    out = dict(_drawn_inputs(seed))
    spreads = {}
    factors = {'hgrn_lb_table': 7.612, 'hgrn_out_norm': 3.49, 'final_norm': 7.726, 'norm_ffn': 5.137}
    for name, (base, spread) in spreads.items():
        noise = np.random.default_rng([zlib.crc32(name.encode()), seed]).standard_normal(out[name].shape)
        drawn = base * np.exp(spread * noise) if base else spread * noise
        out[name] = __import__('jax').numpy.asarray(drawn.astype(out[name].dtype))
    for name, factor in factors.items():
        out[name] = (out[name] * factor).astype(out[name].dtype)
    return out
```

```python
from contextlib import ExitStack

import concourse.bass as bass
from concourse import mybir

F32 = mybir.dt.float32
F32R = mybir.dt.float32r
U8 = mybir.dt.uint8
ALU = mybir.AluOpType
ACT = mybir.ActivationFunctionType

P = 128
D = 2048
T = 256
FF = 5632
TAPS = 3
EPS = 1e-6
DT = D // P
FT = FF // P
HEADS = 16
TG = 4
GC = TG * P
KC = 2
RING = 4
STAGES = 2
SETS = 2
LEVELS = [1, 2, 4, 8, 16, 32, 64, 128]

NORM_MIX, NORM_FFN, LB, OUT_NORM = 0, 2 * DT, 4 * DT, 7 * DT
SC_CONV = 8 * DT
FINAL = SC_CONV + TAPS * DT
FFN_CONV = FINAL + DT
FFN_ROWS = 2 * TAPS * 2 * FT
PARS = FFN_CONV + FFN_ROWS


class Phase:

    def __init__(self, before, n, groups, k_tiles):
        self.n, self.groups, self.cpg = n, groups, k_tiles // KC
        self.cpi = groups * self.cpg
        self.c0 = before.c0 + before.n * before.cpi if before else 0
        self.g0 = before.g0 + before.n * before.groups if before else 0
        assert self.cpi % RING == 0 and self.c0 % RING == 0 and groups % SETS == 0


HGRN_IN = Phase(None, 4, 4, DT)
HGRN_OUT = Phase(HGRN_IN, 2, 2, DT)
UP0 = Phase(HGRN_OUT, 11, 2, DT)
DOWN0 = Phase(UP0, 2, 2, FT)
SC_IN = Phase(DOWN0, 2, 6, DT)
SC_OUT = Phase(SC_IN, 2, 2, DT)
UP1 = Phase(SC_OUT, 11, 2, DT)
DOWN1 = Phase(UP1, 2, 2, FT)
CHUNKS = DOWN1.c0 + DOWN1.n * DOWN1.cpi

S_PAR, S_X = 0, 1
S_RS_HGRN = S_X + DT // TG
S_HGRN = S_RS_HGRN + 1
HGRN_STAGES = 12
S_RS_OUT = S_HGRN + HGRN_STAGES * HGRN_IN.n
S_RS_UP0, S_RS_SC, S_RS_UP1, S_RS_END = (S_RS_OUT + n for n in (1, 2, 3, 4))
S_Y = S_RS_END + 1


def loop(e, phase, body, peel_last=False):
    body(0, True)
    end = phase.n - peel_last
    if end > 2:
        with e.Fori(1, end) as i:
            body(i, False)
    elif end == 2:
        body(1, False)
    if peel_last:
        body(phase.n - 1, False)


def trunk(nc, x, norm_mix, norm_ffn, hgrn_w_in, hgrn_lb_table, hgrn_out_norm, hgrn_w_out, sc_w_in, sc_conv,
          sc_w_out, ffn_w_up, ffn_conv, ffn_w_down, final_norm, identity, level_masks, out):
    with ExitStack() as ctx:
        def sb(name, shape, dt=F32):
            return ctx.enter_context(nc.sbuf_tensor(name, shape, dt))

        def sem(name):
            return ctx.enter_context(nc.semaphore(name))

        with nc.sbuf_tensor("act", [P, FT, 2, T], F32R) as act:
            pass
        act_low = sb("act_low", [P, DT, 2, T], F32R)
        scratch_at = ExitStack()

        def scratch(name, shape, dt=F32):
            return scratch_at.enter_context(nc.sbuf_tensor(name, shape, dt))

        fpre = scratch("fpre", [P, TG, T])
        suf = scratch("suf", [P, TG, T])
        qh = scratch("qh", [P, TG, T])
        kh = scratch("kh", [P, TG, T])
        ql = scratch("ql", [P, 2, TG, T])
        kl = scratch("kl", [P, 2, TG, T])
        vh = scratch("vh", [P, TG, T])
        vt = scratch("vt", [P, TG, 2, P])
        a_diag = scratch("a_diag", [P, TG, 2, P])
        a_off = scratch("a_off", [P, TG, P])
        o_sb = scratch("o_sb", [P, TG, T])
        scratch_at.close()
        x_tok = scratch("x_tok", [P, T // P, D])
        rows = scratch("rows", [P, 7, P])
        masks_f32 = scratch("masks_f32", [P, len(LEVELS), P])
        scratch_at.close()
        act_high = sb("act_high", [P, FT - DT, 2, T], F32R)

        h = sb("h", [P, DT, T])
        xn = sb("xn", [P, DT, 2, T], F32R)
        raw = sb("raw", [P, RING, KC, GC])
        w_hi = sb("w_hi", [P, RING, KC, GC], F32R)
        w_lo = sb("w_lo", [P, RING, KC, GC], F32R)
        pad = sb("pad", [P, TG, T + TAPS - 1])
        ta = sb("ta", [P, TG, T])
        tb = sb("tb", [P, TG, T])
        sq_acc = sb("sq_acc", [P, 2, T])
        std = sb("std", [P, T])
        rs = sb("rs", [P, T])
        par = sb("par", [P, PARS])
        lb = sb("lb", [P, HEADS])
        one_less_lb = sb("one_less_lb", [P, HEADS])
        lb_max = sb("lb_max", [P, HEADS])
        lb_exp = sb("lb_exp", [P, 3, HEADS])
        ident = sb("ident", [P, P])
        ones = sb("ones", [P, P])
        masks = sb("masks", [P, len(LEVELS), P], U8)

        acc = ctx.enter_context(nc.psum_tensor("acc", [P, SETS, TG, T], F32))
        side = ctx.enter_context(nc.psum_tensor("side", [P, STAGES, TG * T], F32))

        w_loaded = [sem(f"w_loaded{n}") for n in range(RING)]
        loads_begun = sem("loads_begun")
        x_loaded, rows_loaded, const_loaded = sem("x_loaded"), sem("rows_loaded"), sem("const_loaded")
        hi_ready = sem("hi_ready")
        lo_ready = sem("lo_ready")
        chunk_used = sem("chunk_used")
        acc_free = sem("acc_free")
        stage_done = sem("stage_done")
        stage_free = sem("stage_free")
        inits = sem("inits")
        chain = sem("chain")
        rs_chain = sem("rs_chain")
        par_ready = sem("par_ready")
        masks_ready = sem("masks_ready")
        lb_max_ready, lb_exp_ready = sem("lb_max_ready"), sem("lb_exp_ready")
        h_ready = sem("h_ready")
        sq_ready = sem("sq_ready")
        sq_sum = sem("sq_sum")
        xhi_ready = sem("xhi_ready")
        xn_ready = sem("xn_ready")
        act_ready = sem("act_ready")
        var_ready, std_ready = sem("var_ready"), sem("std_ready")
        gate_in, gate_sig = sem("gate_in"), sem("gate_sig")
        conv_ready, silu_ready = sem("conv_ready"), sem("silu_ready")
        qk_ready = sem("qk_ready")
        v_ready, a_ready = sem("v_ready"), sem("a_ready")
        o_ready = sem("o_ready")
        y_ready, y_tok_ready = sem("y_ready"), sem("y_tok_ready")
        y_stored = [sem("y_stored0"), sem("y_stored1")]

        block = ctx.enter_context(nc.Block())

        def at(i, per, first):
            return i * per + first

        def rows_of(w, kk, col):
            return w[kk * KC * P:(kk + 1) * KC * P, bass.ds(col, GC)].rearrange("(k p) n -> p k n", p=P)

        @block.sync
        def _(sp):
            def stream(phase, w, column):
                def body(i, first):
                    for g in range(phase.groups):
                        for kk in range(phase.cpg):
                            c = phase.c0 + g * phase.cpg + kk
                            sp.wait_ge(lo_ready, at(i, phase.cpi, c + 1))
                            sp.sem_inc(loads_begun, 1)
                            sp.dma_start(raw[:, c % RING], rows_of(w, kk, column(i, g))) \
                                .then_inc(w_loaded[c % RING], 16)
                with sp.Fori(0, phase.n) as i:
                    body(i, False)

            stream(HGRN_IN, hgrn_w_in[0], lambda i, g: i * GC + [D, 0, 2 * D, 3 * D][g])
            stream(HGRN_OUT, hgrn_w_out[0], lambda i, g: i * (2 * GC) + g * GC)
            stream(UP0, ffn_w_up[0], lambda i, g: i * GC + g * FF)
            stream(DOWN0, ffn_w_down[0], lambda i, g: i * (2 * GC) + g * GC)
            stream(SC_IN, sc_w_in[0], lambda i, g: i * (2 * GC) + (g // 3) * GC + [D, 2 * D, 0][g % 3])
            stream(SC_OUT, sc_w_out[0], lambda i, g: i * (2 * GC) + g * GC)
            stream(UP1, ffn_w_up[1], lambda i, g: i * GC + g * FF)
            stream(DOWN1, ffn_w_down[1], lambda i, g: i * (2 * GC) + g * GC)
            y = out[0].rearrange("(b p) n -> p b n", p=P)
            for n in range(DT // TG):
                sp.wait_ge(y_tok_ready, n + 1)
                sp.dma_start(y[:, :, n * GC:(n + 1) * GC], [ta, tb][n % 2][:, :, :].rearrange(
                    "p (b j) t -> p b (j t)", b=2)).then_inc(y_stored[n % 2], 16)
            for s in y_stored:
                sp.wait_ge(s, 16 * (DT // TG // 2))

        @block.gpsimd
        def _(pool):
            for t in (ones, sq_acc, pad):
                nc.gpsimd.memset(t[:], 1.0 if t is ones else 0.0).then_inc(inits, 1)
            pool.wait_ge(xn_ready, DT // TG)
            pool.wait_ge(masks_ready, 1)
            for t in (ql, kl, a_diag):
                nc.gpsimd.memset(t[:], 0.0).then_inc(inits, 1)

        @block.scalar
        def _(act_e):
            act_e.dma_start(ident[:], identity).then_inc(const_loaded, 16)
            act_e.dma_start(masks_f32[:], level_masks.rearrange("p (l t) -> p l t", t=P)).then_inc(const_loaded, 16)
            n = 0
            for w, tile in ((norm_mix, 0), (norm_ffn, 0), (hgrn_lb_table, 0), (hgrn_out_norm, 0), (sc_conv, 1)):
                if tile and n == P:
                    n = 0
                a = w.rearrange("a (t p) -> (a t) p", p=P) if len(w.shape) == 2 else \
                    w.rearrange("l a (t p) -> (l a t) p", p=P)
                act_e.dma_start(rows[n:n + a.shape[0], tile, :], a).then_inc(rows_loaded, 16)
                n += a.shape[0]
            act_e.dma_start(rows[n:n + DT, 1, :], final_norm.rearrange("(t p) -> t p", p=P)).then_inc(rows_loaded, 16)
            fc = ffn_conv.rearrange("l a (t p) -> (l a t) p", p=P)
            act_e.dma_start(rows[:, 2:6, :], fc[0:4 * P, :].rearrange("(t p) n -> p t n", p=P)).then_inc(rows_loaded, 16)
            act_e.dma_start(rows[0:FFN_ROWS - 4 * P, 6, :], fc[4 * P:FFN_ROWS, :]).then_inc(rows_loaded, 16)
            act_e.dma_start(x_tok[:], x[0].rearrange("(b p) n -> p b n", p=P)).then_inc(x_loaded, 16)

            def split(i, phase, c):
                act_e.wait_ge(w_loaded[c % RING], at(i, 4 * phase.cpi, 16 * (c // RING + 1)))
                act_e.wait_ge(chunk_used, at(i, phase.cpi, c + 1))
                nc.scalar.activation(w_hi[:, c % RING], raw[:, c % RING], ACT.Copy).then_inc(hi_ready, 1)

            def phase_of(phase, pieces, peel_last=False):
                def body(i, first):
                    for g in range(phase.groups):
                        for kk in range(phase.cpg):
                            c = phase.c0 + g * phase.cpg + kk
                            last = isinstance(i, int) and i * phase.cpi + c + RING >= CHUNKS
                            if not last:
                                split(i, phase, c + RING)
                            pieces(i, first, g, kk)
                loop(act_e, phase, body, peel_last)

            def root(n):
                act_e.wait_ge(var_ready, n + 1)
                nc.scalar.activation(std[:], std[:], ACT.Sqrt).then_inc(std_ready, 1)

            def squares(r, src, dst, i=0, per=0):
                act_e.wait_ge(h_ready, at(i, per, r + 1))
                nc.scalar.activation(dst, src, ACT.Square).then_inc(sq_ready, 1)

            def residual(i, per, r, tile, weight):
                act_e.wait_ge(h_ready, at(i, per, r + 1))
                nc.scalar.activation(ta[:], h[:, bass.ds(tile, TG), :], ACT.Square).then_inc(sq_ready, 1)
                if weight is None:
                    return
                for j in range(TG):
                    o = nc.scalar.activation(xn[:, bass.ds(tile + j, 1), 0, :], h[:, bass.ds(tile + j, 1), :],
                                             ACT.Copy, scale=par[:, bass.ds(weight + tile + j, 1)])
                o.then_inc(xhi_ready, 1)

            def residual_phase(phase, r0, weight, rs_n=None, peel_last=False):
                def pieces(i, first, g, kk):
                    if rs_n is not None and first and (g, kk) == (0, RING):
                        root(rs_n)
                    if kk == phase.cpg - 1:
                        residual(i, 2, r0 + g, i * (2 * TG) + g * TG, weight)
                phase_of(phase, pieces, peel_last)

            def up_phase(phase, n, rs_n):
                def pieces(i, first, g, kk):
                    if first and (g, kk) == (0, RING):
                        root(rs_n)
                    if g == 0 and kk == phase.cpg - 1:
                        act_e.wait_ge(conv_ready, at(i, 1, n + 1))
                        nc.scalar.activation(ta[:], ta[:], ACT.Silu).then_inc(silu_ready, 1)
                phase_of(phase, pieces)

            for c in range(RING):
                split(0, HGRN_IN, c)
            act_e.wait_ge(lb_max_ready, 1)
            nc.scalar.activation(lb_exp[:], lb_exp[:], ACT.Exp).then_inc(lb_exp_ready, 1)
            act_e.wait_ge(par_ready, 1)
            for g in range(DT // TG):
                residual(0, 0, g, g * TG, NORM_MIX)

            def hgrn(i, first, g, kk):
                if first and (g, kk) == (0, RING):
                    root(0)
                if (g, kk) in ((1, 0), (2, 0), (3, HGRN_IN.cpg - 1)):
                    act_e.wait_ge(gate_in, at(i, 3, {1: 1, 2: 2, 3: 3}[g]))
                    nc.scalar.activation(tb[:], ta[:], ACT.Sigmoid).then_inc(gate_sig, 1)
                if (g, kk) == (3, HGRN_IN.cpg - 1):
                    act_e.wait_ge(o_ready, at(i, 1, 1))
                    nc.scalar.activation(qh[:], o_sb[:], ACT.Square).then_inc(sq_ready, 1)

            phase_of(HGRN_IN, hgrn)
            residual_phase(HGRN_OUT, 4, NORM_FFN, rs_n=1)
            up_phase(UP0, 0, 2)
            residual_phase(DOWN0, 8, NORM_MIX + DT)

            def sc(i, first, g, kk):
                if first and (g, kk) == (0, RING):
                    root(3)
            phase_of(SC_IN, sc)
            residual_phase(SC_OUT, 12, NORM_FFN + DT)
            up_phase(UP1, UP0.n, 4)
            residual_phase(DOWN1, 16, None, peel_last=True)
            root(5)

        @block.vector
        def _(dve):
            v = nc.vector
            links = [0, 0, 0]

            def link(ins, i):
                links[2] += 1
                ins.then_inc(chain, 1)
                dve.wait_ge(chain, at(i, links[1], links[0] + links[2]))

            def phase_of(phase, pieces, peel_last=False):
                def body(i, first):
                    if links[1] == 0:
                        assert first
                    links[2] = 0
                    if peel_last and not first and isinstance(i, int):
                        pass
                    for g in range(phase.groups):
                        for kk in range(phase.cpg):
                            c = phase.c0 + g * phase.cpg + kk
                            last = isinstance(i, int) and i * phase.cpi + c + RING >= CHUNKS
                            if not last:
                                split(i, phase, c + RING)
                            pieces(i, first, g, kk)
                    if first:
                        links[1] = links[2]
                    assert links[1] == links[2]
                links[1] = 0
                loop(dve, phase, body, peel_last)
                links[0] += phase.n * links[1]
                links[1] = links[2] = 0

            def split(i, phase, c):
                dve.wait_ge(w_loaded[c % RING], at(i, 4 * phase.cpi, 16 * (c // RING + 1)))
                dve.wait_ge(hi_ready, at(i, phase.cpi, c + 1))
                dve.wait_ge(chunk_used, at(i, phase.cpi, c + 1))
                v.tensor_tensor(w_lo[:, c % RING], raw[:, c % RING], w_hi[:, c % RING].bitcast(F32),
                                ALU.subtract).then_inc(lo_ready, 1)

            steps = [0]

            def then(ins):
                steps[0] += 1
                ins.then_inc(rs_chain, 1)
                dve.wait_ge(rs_chain, steps[0])

            def rms(n, stage):
                dve.wait_ge(stage_done, stage + 1)
                v.memset(sq_acc[:], 0.0)
                v.tensor_scalar(std[:], side[:, stage % STAGES, 0:T], 1.0 / D, EPS, ALU.mult, ALU.add) \
                    .then_inc(var_ready, 1)
                dve.wait_ge(var_ready, n + 1)
                v.sem_inc(stage_free, 1)
                dve.wait_ge(std_ready, n + 1)
                then(v.reciprocal(rs[:], std[:]))

            def scaled(i, phase, g, dst):
                dve.wait_ge(chunk_used, at(i, phase.cpi, phase.c0 + (g + 1) * phase.cpg + RING))
                link(v.tensor_tensor(dst, acc[:, g % SETS], rs[:, None, :].to_broadcast([P, TG, T]), ALU.mult), i)
                v.sem_inc(acc_free, 1)

            def add_squares(i, per, n, src):
                dve.wait_ge(sq_ready, at(i, per, n + 1))
                link(v.tensor_tensor(sq_acc[:], sq_acc[:], src[:, 0:2, :], ALU.add), i)
                v.tensor_tensor(sq_acc[:], sq_acc[:], src[:, 2:4, :], ALU.add).then_inc(sq_sum, 1)

            def low_parts(i, per, r, tile, weight):
                dve.wait_ge(xhi_ready, at(i, per, r + 1))
                for j in range(TG):
                    o = v.scalar_tensor_tensor(out=xn[:, bass.ds(tile + j, 1), 1, :], in0=h[:, bass.ds(tile + j, 1), :],
                                               scalar=par[:, bass.ds(weight + tile + j, 1)],
                                               in1=xn[:, bass.ds(tile + j, 1), 0, :].bitcast(F32),
                                               op0=ALU.mult, op1=ALU.subtract)
                o.then_inc(xn_ready, 1)

            def split_act(i, tile, src):
                dst = act[:, bass.ds(tile, TG), :, :]
                link(v.tensor_copy(dst[:, :, 0, :], src), i)
                v.tensor_tensor(dst[:, :, 1, :], src, dst[:, :, 0, :].bitcast(F32), ALU.subtract).then_inc(act_ready, 1)

            def convolve(i, dst, column, step):
                for tap in reversed(range(TAPS)):
                    for j in range(TG):
                        w = par[:, bass.ds(column + tap * step + j, 1)]
                        src = pad[:, j, tap:tap + T]
                        if tap == TAPS - 1:
                            o = v.tensor_scalar(dst[:, j, :], src, w, None, ALU.mult)
                        else:
                            o = v.scalar_tensor_tensor(out=dst[:, j, :], in0=src, scalar=w, in1=dst[:, j, :],
                                                       op0=ALU.mult, op1=ALU.add)
                    if tap:
                        link(o, i)
                return o

            def residual_phase(phase, r0, sq0, weight, rs_n=None, rs_stage=None, peel_last=False):
                def pieces(i, first, g, kk):
                    if rs_n is not None and first and (g, kk) == (0, RING):
                        rms(rs_n, rs_stage)
                    if kk != phase.cpg - 1:
                        return
                    tile = i * (2 * TG) + g * TG
                    dst = h[:, bass.ds(tile, TG), :]
                    if rs_n is not None:
                        scaled(i, phase, g, tb[:])
                        v.tensor_tensor(dst, dst, tb[:], ALU.add).then_inc(h_ready, 1)
                        dve.wait_ge(h_ready, at(i, 2, r0 + g + 1))
                    else:
                        dve.wait_ge(chunk_used, at(i, phase.cpi, phase.c0 + (g + 1) * phase.cpg + RING))
                        v.tensor_tensor(dst, dst, acc[:, g % SETS], ALU.add).then_inc(h_ready, 1)
                        dve.wait_ge(h_ready, at(i, 2, r0 + g + 1))
                        v.sem_inc(acc_free, 1)
                    add_squares(i, 2, sq0 + g, ta)
                    if weight is not None:
                        low_parts(i, 2, r0 + g, tile, weight)
                phase_of(phase, pieces, peel_last)

            def up_phase(phase, n, rs_n, rs_stage, conv):
                def pieces(i, first, g, kk):
                    if first and (g, kk) == (0, RING):
                        rms(rs_n, rs_stage)
                    if kk != phase.cpg - 1:
                        return
                    scaled(i, phase, g, pad[:, :, TAPS - 1:])
                    if g == 0:
                        convolve(i, ta, conv + i * TG, 2 * FT).then_inc(conv_ready, 1)
                    else:
                        link(convolve(i, tb, conv + FT + i * TG, 2 * FT), i)
                        dve.wait_ge(silu_ready, at(i, 1, n + 1))
                        link(v.tensor_tensor(tb[:], ta[:], tb[:], ALU.mult), i)
                        split_act(i, i * TG, tb[:])
                phase_of(phase, pieces)

            v.sem_inc(lo_ready, RING)
            v.sem_inc(acc_free, SETS)
            v.sem_inc(stage_free, STAGES)
            for c in range(RING):
                split(0, HGRN_IN, c)

            dve.wait_ge(const_loaded, 32)
            v.tensor_copy(masks[:], masks_f32[:]).then_inc(masks_ready, 1)

            dve.wait_ge(stage_done, S_PAR + 1)
            v.tensor_copy(par[:, 0:SC_CONV], side[:, S_PAR % STAGES, 0:P])
            v.tensor_copy(par[:, SC_CONV:FFN_CONV], side[:, S_PAR % STAGES, P:P + 4 * DT])
            v.tensor_copy(par[:, FFN_CONV:PARS], side[:, S_PAR % STAGES, 2 * P:2 * P + FFN_ROWS]).then_inc(par_ready, 1)
            dve.wait_ge(par_ready, 1)
            v.sem_inc(stage_free, 1)
            table = par[:, LB:LB + 3 * HEADS].rearrange("p (r h) -> p r h", r=3)
            then(v.tensor_tensor(lb_max[:], table[:, 0], table[:, 1], ALU.max))
            then(v.tensor_tensor(lb_max[:], lb_max[:], table[:, 2], ALU.max))
            v.tensor_tensor(lb_exp[:], table, lb_max[:, None, :].to_broadcast([P, 3, HEADS]), ALU.subtract) \
                .then_inc(lb_max_ready, 1)
            dve.wait_ge(lb_exp_ready, 1)
            then(v.tensor_tensor(lb_max[:], lb_exp[:, 0], lb_exp[:, 1], ALU.add))
            then(v.tensor_tensor(lb_max[:], lb_max[:], lb_exp[:, 2], ALU.add))
            then(v.reciprocal(lb_max[:], lb_max[:]))
            then(v.tensor_tensor(lb[:], lb_exp[:, 0], lb_max[:], ALU.mult))
            then(v.tensor_scalar(one_less_lb[:], lb[:], -1.0, 1.0, ALU.mult, ALU.add))

            dve.wait_ge(inits, 3)
            for g in range(DT // TG):
                s = S_X + g
                dve.wait_ge(stage_done, s + 1)
                v.tensor_copy(h[:, g * TG:(g + 1) * TG, :], side[:, s % STAGES].rearrange("p (j t) -> p j t", j=TG)) \
                    .then_inc(h_ready, 1)
                dve.wait_ge(h_ready, g + 1)
                v.sem_inc(stage_free, 1)
                dve.wait_ge(sq_ready, g + 1)
                then(v.tensor_tensor(sq_acc[:], sq_acc[:], ta[:, 0:2, :], ALU.add))
                then(v.tensor_tensor(sq_acc[:], sq_acc[:], ta[:, 2:4, :], ALU.add))
                v.sem_inc(sq_sum, 1)
                low_parts(0, 0, g, g * TG, NORM_MIX)
            dve.wait_ge(inits, 6)

            last = HGRN_IN.cpg - 1

            def halves(t, n):
                return t.rearrange("p j (b z n) -> p (j b) z n", z=2, n=n)

            def level_operands(i, m):
                n = LEVELS[m]
                pre, su = halves(fpre[:], n), halves(suf[:], n)
                buf = m % 2
                if n == 1:
                    v.tensor_tensor(halves(ql[:, buf], n)[:, :, 1], halves(qh[:], n)[:, :, 1], pre[:, :, 1], ALU.mult) \
                        .then_inc(qk_ready, 1)
                    v.memset(su[:, :, 1], 1.0)
                    link(v.tensor_copy(su[:, :, 0], pre[:, :, 1]), i)
                else:
                    v.tensor_tensor(halves(ql[:, buf], n)[:, :, 1], halves(qh[:], n)[:, :, 1], pre[:, :, 1], ALU.mult)
                    v.tensor_tensor(halves(kl[:, buf], n)[:, :, 0], halves(kh[:], n)[:, :, 0], su[:, :, 0], ALU.mult) \
                        .then_inc(qk_ready, 1)
                    if m == len(LEVELS) - 1:
                        return
                    shape = [P, TG * T // (2 * n), n]
                    link(v.tensor_tensor(su[:, :, 0], su[:, :, 0], pre[:, :, 1, n - 1:n].to_broadcast(shape),
                                         ALU.mult), i)
                shape = [P, TG * T // (2 * n), n]
                link(v.tensor_tensor(pre[:, :, 1], pre[:, :, 1], pre[:, :, 0, n - 1:n].to_broadcast(shape), ALU.mult), i)

            def take_stage(i, j):
                s = S_HGRN + j
                src = side[:, s % STAGES]
                if j == 11:
                    dve.wait_ge(stage_done, at(i, HGRN_STAGES, s + 1))
                if j < 8:
                    mask = masks[:, j:j + 1, :].to_broadcast([P, 2 * TG, P])
                    o = v.copy_predicated(a_diag[:].rearrange("p j b t -> p (j b) t"), mask,
                                          src.rearrange("p (n t) -> p n t", t=P))
                elif j == 8:
                    o = v.tensor_copy(a_off[:], src[:, 0:TG * P].rearrange("p (j t) -> p j t", j=TG))
                elif j < 11:
                    c = 2 * (j - 9)
                    o = v.tensor_copy(vt[:, c:c + 2], src[:, 0:4 * P].rearrange("p (j b d) -> p j b d", j=2, b=2))
                else:
                    o = v.tensor_copy(o_sb[:], src.rearrange("p (j t) -> p j t", j=TG))
                link(o, i)
                v.sem_inc(stage_free, 1)
                if j in (8, 10):
                    v.sem_inc(a_ready, 1)
                if j == 11:
                    v.sem_inc(o_ready, 1)

            def hgrn(i, first, g, kk):
                n = g * HGRN_IN.cpg + kk - 2 * HGRN_IN.cpg
                if first and (g, kk) == (0, RING):
                    rms(0, S_RS_HGRN)
                if kk == last and g in (0, 1, 3):
                    scaled(i, HGRN_IN, g, ta[:])
                    v.sem_inc(gate_in, 1)
                if kk == last and g == 2:
                    scaled(i, HGRN_IN, g, vh[:])
                    v.sem_inc(v_ready, 1)
                if (g, kk) == (1, 0):
                    dve.wait_ge(gate_sig, at(i, 3, 1))
                    for j in range(TG):
                        c = bass.ds(i * TG + j, 1)
                        o = v.tensor_scalar(fpre[:, j, :], tb[:, j, :], one_less_lb[:, c], lb[:, c], ALU.mult, ALU.add)
                    link(o, i)
                    v.tensor_scalar(kh[:], fpre[:], -1.0, 1.0, ALU.mult, ALU.add)
                if n >= 2 and n - 2 <= 10:
                    take_stage(i, n - 2)
                if n == 0:
                    dve.wait_ge(gate_sig, at(i, 3, 2))
                    link(v.scalar_tensor_tensor(out=qh[:], in0=ta[:], scalar=float(P) ** -0.5, in1=tb[:],
                                                op0=ALU.mult, op1=ALU.mult), i)
                    v.sem_inc(qk_ready, 1)
                if 1 <= n <= len(LEVELS):
                    level_operands(i, n - 1)
                if (g, kk) == (3, last):
                    take_stage(i, 11)
                    dve.wait_ge(gate_sig, at(i, 3, 3))
                    link(v.tensor_tensor(tb[:], ta[:], tb[:], ALU.mult), i)
                    for j in range(TG):
                        o = v.scalar_tensor_tensor(out=tb[:, j, :], in0=o_sb[:, j, :],
                                                   scalar=par[:, bass.ds(OUT_NORM + i * TG + j, 1)], in1=tb[:, j, :],
                                                   op0=ALU.mult, op1=ALU.mult)
                    link(o, i)
                    split_act(i, i * TG, tb[:])
                    add_squares(i, 1, 4, qh)

            phase_of(HGRN_IN, hgrn)
            residual_phase(HGRN_OUT, 4, 8, NORM_FFN, 1, S_RS_OUT)
            up_phase(UP0, 0, 2, S_RS_UP0, FFN_CONV)
            residual_phase(DOWN0, 8, 12, NORM_MIX + DT)

            def sc(i, first, g, kk):
                if first and (g, kk) == (0, RING):
                    rms(3, S_RS_SC)
                if kk != last:
                    return
                tile = i * (2 * TG) + (g // 3) * TG
                if g % 3 == 0:
                    scaled(i, SC_IN, g, ta[:])
                elif g % 3 == 1:
                    u = pad[:, :, TAPS - 1:]
                    scaled(i, SC_IN, g, u)
                    link(v.tensor_tensor(u, u, ta[:], ALU.mult), i)
                    link(convolve(i, tb, SC_CONV + tile, DT), i)
                else:
                    scaled(i, SC_IN, g, ta[:])
                    link(v.tensor_tensor(tb[:], ta[:], tb[:], ALU.mult), i)
                    split_act(i, tile, tb[:])

            phase_of(SC_IN, sc)
            residual_phase(SC_OUT, 12, 16, NORM_FFN + DT)
            up_phase(UP1, UP0.n, 4, S_RS_UP1, FFN_CONV + TAPS * 2 * FT)
            residual_phase(DOWN1, 16, 20, None, peel_last=True)

            rms(5, S_RS_END)
            for j in range(DT):
                o = v.scalar_tensor_tensor(out=h[:, j, :], in0=h[:, j, :], scalar=par[:, FINAL + j:FINAL + j + 1],
                                           in1=rs[:], op0=ALU.mult, op1=ALU.mult)
                if j % TG == TG - 1:
                    o.then_inc(y_ready, 1)
            for n in range(DT // TG):
                s = S_Y + n
                dve.wait_ge(stage_done, s + 1)
                if n >= 2:
                    dve.wait_ge(y_stored[n % 2], 16)
                v.tensor_copy([ta, tb][n % 2][:].rearrange("p j t -> p (j t)"), side[:, s % STAGES]) \
                    .then_inc(y_tok_ready, 1)
                dve.wait_ge(y_tok_ready, n + 1)
                v.sem_inc(stage_free, 1)

        @block.tensor
        def _(pe):
            mm = nc.tensor.matmul

            def stage(s, steps, i=0, per=0):
                pe.wait_ge(stage_free, at(i, per, s + 1))
                for step in steps:
                    o = step(side[:, s % STAGES])
                o.then_inc(stage_done, 1)

            def turn(src, column, n=P):
                return lambda to: nc.tensor.transpose(to[:, column:column + n], src, ident[0:n, 0:n])

            def sum_squares(n, s):
                pe.wait_ge(sq_sum, DT // TG * (n + 1))
                stage(s, [lambda to, j=j: mm(to[:, 0:T], ones[:], sq_acc[:, j, :], start=(j == 0), stop=(j == 1))
                          for j in range(2)])

            def phase_of(phase, src, ready, ready0, rs=None, pieces=None):
                def body(i, first):
                    for g in range(phase.groups):
                        to = acc[:, g % SETS]
                        for kk in range(phase.cpg):
                            c = phase.c0 + g * phase.cpg + kk
                            if kk == 0:
                                pe.wait_ge(acc_free, at(i, phase.groups, phase.g0 + g + 1))
                            if first and g == 0 and kk * KC % TG == 0:
                                pe.wait_ge(ready, ready0 + kk * KC // TG + 1)
                            pe.wait_ge(hi_ready, at(i, phase.cpi, c + 1))
                            pe.wait_ge(lo_ready, at(i, phase.cpi, c + 1 + RING))
                            for k in range(KC):
                                t = kk * KC + k
                                begin, end = t == 0, t == phase.cpg * KC - 1
                                for j in range(TG):
                                    hi, lo = (w[:, c % RING, k, j * P:(j + 1) * P] for w in (w_hi, w_lo))
                                    mm(to[:, j, :], hi, src[:, t, 0, :], start=begin and j % 2 == 0, stop=False,
                                       skip_group_check=True)
                                    mm(to[:, j, :], hi, src[:, t, 1, :], start=False, stop=False, skip_group_check=True)
                                    o = mm(to[:, j, :], lo, src[:, t, 0, :], start=False, stop=end, skip_group_check=True)
                            o.then_inc(chunk_used, 1)
                            if first and rs and (g, kk) == (0, RING):
                                sum_squares(*rs)
                            if pieces:
                                pieces(i, g, kk)
                loop(pe, phase, body)

            pe.sem_inc(chunk_used, RING)
            pe.wait_ge(const_loaded, 32)
            pe.wait_ge(rows_loaded, 16 * 8)
            stage(S_PAR, [turn(rows[:, 0, :], 0), turn(rows[0:4 * DT, 1, :], P, 4 * DT)] +
                  [turn(rows[:, 2 + t, :], (2 + t) * P) for t in range(4)] +
                  [turn(rows[0:FFN_ROWS - 4 * P, 6, :], 6 * P, FFN_ROWS - 4 * P)])
            pe.wait_ge(x_loaded, 16)
            for g in range(DT // TG):
                stage(S_X + g, [turn(x_tok[:, b, (g * TG + j) * P:(g * TG + j + 1) * P], j * T + b * P)
                                for j in range(TG) for b in range(T // P)])
            pe.wait_ge(inits, 3)

            def hgrn(i, g, kk):
                n = g * HGRN_IN.cpg + kk - 2 * HGRN_IN.cpg
                s = S_HGRN + n - 1
                if 1 <= n <= 9:
                    m = n - 2
                    lhs = kh[:] if m < 1 else kl[:, m % 2]
                    rhs = qh[:] if m < 0 else ql[:, m % 2]
                    pe.wait_ge(qk_ready, at(i, 9, n))
                    if m < len(LEVELS) - 1:
                        steps = [lambda to, j=j, b=b: mm(to[:, (2 * j + b) * P:(2 * j + b + 1) * P],
                                                         lhs[:, j, b * P:(b + 1) * P], rhs[:, j, b * P:(b + 1) * P],
                                                         start=True, stop=True)
                                 for j in range(TG) for b in range(2)]
                    else:
                        steps = [lambda to, j=j: mm(to[:, j * P:(j + 1) * P], lhs[:, j, 0:P], rhs[:, j, P:T],
                                                    start=True, stop=True) for j in range(TG)]
                    stage(s, steps, i, HGRN_STAGES)
                elif n in (10, 11):
                    if n == 10:
                        pe.wait_ge(v_ready, at(i, 1, 1))
                    j0 = 2 * (n - 10)
                    stage(s, [turn(vh[:, j0 + j, b * P:(b + 1) * P], (2 * j + b) * P) for j in range(2) for b in range(2)],
                          i, HGRN_STAGES)
                elif (g, kk) == (3, HGRN_IN.cpg - 1):
                    pe.wait_ge(a_ready, at(i, 2, 2))
                    steps = []
                    for j in range(TG):
                        for b, a, col, begin, end in ((0, a_diag[:, j, 0], 0, j % 2 == 0, True),
                                                      (0, a_off[:, j], P, False, False),
                                                      (1, a_diag[:, j, 1], P, False, True)):
                            steps.append(lambda to, j=j, b=b, a=a, col=col, begin=begin, end=end: mm(
                                to[:, j * T + col:j * T + col + P], vt[:, j, b], a, start=begin, stop=end,
                                skip_group_check=True))
                    stage(S_HGRN + 11, steps, i, HGRN_STAGES)

            G = DT // TG
            phase_of(HGRN_IN, xn, xn_ready, 0, (0, S_RS_HGRN), hgrn)
            phase_of(HGRN_OUT, act, act_ready, 0, (1, S_RS_OUT))
            phase_of(UP0, xn, xn_ready, G, (2, S_RS_UP0))
            phase_of(DOWN0, act, act_ready, G)
            phase_of(SC_IN, xn, xn_ready, 2 * G, (3, S_RS_SC))
            phase_of(SC_OUT, act, act_ready, G + UP0.n)
            phase_of(UP1, xn, xn_ready, 3 * G, (4, S_RS_UP1))
            phase_of(DOWN1, act, act_ready, 2 * G + UP0.n)
            sum_squares(5, S_RS_END)
            for n in range(DT // TG):
                pe.wait_ge(y_ready, n + 1)
                stage(S_Y + n, [turn(h[:, n * TG + j, b * P:(b + 1) * P], (b * TG + j) * P)
                                for b in range(T // P) for j in range(TG)])


_INS = ["x", "norm_mix", "norm_ffn", "hgrn_w_in", "hgrn_lb_table", "hgrn_out_norm", "hgrn_w_out", "sc_w_in",
        "sc_conv", "sc_w_out", "ffn_w_up", "ffn_conv", "ffn_w_down", "final_norm"]


def kernel(**inputs):
    import numpy as np
    import concourse.bacc as bacc
    from concourse.bass_utils import run_bass_kernel_spmd

    nc = bacc.Bacc("TRN2", target_bir_lowering=False, num_devices=1)
    arrays = {f"in_{name}": np.ascontiguousarray(inputs[name]) for name in _INS}
    s, t = np.arange(P)[:, None, None], np.arange(P)[None, None, :]
    n = np.array(LEVELS[:-1])[None, :, None]
    pairs = (s // (2 * n) == t // (2 * n)) & (s // n % 2 == 0) & (t // n % 2 == 1)
    arrays["in_identity"] = np.eye(P, dtype=np.float32)
    arrays["in_level_masks"] = np.concatenate([s == t, pairs], axis=1).astype(np.float32).reshape(P, -1)
    args = [nc.dram_tensor(k, a.shape, mybir.dt.from_np(a.dtype), kind="ExternalInput").ap() for k, a in arrays.items()]
    args.append(nc.dram_tensor("out", (1, T, D), F32, kind="ExternalOutput").ap())
    trunk(nc, *args)
    return run_bass_kernel_spmd(nc, [arrays], core_ids=[0]).results[0]["out"]
```

```python
from contextlib import ExitStack

import concourse.bass as bass
from concourse import mybir

F32 = mybir.dt.float32
F32R = mybir.dt.float32r
U8 = mybir.dt.uint8
ALU = mybir.AluOpType
ACT = mybir.ActivationFunctionType

P = 128
D = 2048
T = 256
FF = 5632
TAPS = 3
EPS = 1e-6
DT = D // P
FT = FF // P
HEADS = 16
TG = 4
GC = TG * P
KC = 2
RING = 4
STAGES = 2
SETS = 2
LEVELS = [1, 2, 4, 8, 16, 32, 64, 128]
HALF = P // 2
MASKS = P + (len(LEVELS) - 1) * HALF

NORM_MIX, NORM_FFN, LB, OUT_NORM = 0, 2 * DT, 4 * DT, 7 * DT
SC_CONV = 8 * DT
FINAL = SC_CONV + TAPS * DT
FFN_CONV = FINAL + DT
FFN_ROWS = 2 * TAPS * 2 * FT
PARS = FFN_CONV + FFN_ROWS


class Phase:

    def __init__(self, before, n, groups, k_tiles):
        self.n, self.groups, self.cpg = n, groups, k_tiles // KC
        self.cpi = groups * self.cpg
        self.c0 = before.c0 + before.n * before.cpi if before else 0
        self.g0 = before.g0 + before.n * before.groups if before else 0
        assert self.cpi % RING == 0 and self.c0 % RING == 0 and groups % SETS == 0


HGRN_IN = Phase(None, 4, 4, DT)
HGRN_OUT = Phase(HGRN_IN, 2, 2, DT)
UP0 = Phase(HGRN_OUT, 11, 2, DT)
DOWN0 = Phase(UP0, 2, 2, FT)
SC_IN = Phase(DOWN0, 2, 6, DT)
SC_OUT = Phase(SC_IN, 2, 2, DT)
UP1 = Phase(SC_OUT, 11, 2, DT)
DOWN1 = Phase(UP1, 2, 2, FT)
CHUNKS = DOWN1.c0 + DOWN1.n * DOWN1.cpi

S_PAR, S_X = 0, 1
S_RS_HGRN = S_X + DT // TG
S_HGRN = S_RS_HGRN + 1
HGRN_STAGES = 12
S_RS_OUT = S_HGRN + HGRN_STAGES * HGRN_IN.n
S_RS_UP0, S_RS_SC, S_RS_UP1, S_Y = (S_RS_OUT + n for n in (1, 2, 3, 4))
S_RS_END = S_Y + DT // TG


def loop(e, phase, body, peel_last=False):
    body(0, True)
    end = phase.n - peel_last
    if end > 2:
        with e.Fori(1, end) as i:
            body(i, False)
    elif end == 2:
        body(1, False)
    if peel_last:
        body(phase.n - 1, False)


def trunk(nc, x, norm_mix, norm_ffn, hgrn_w_in, hgrn_lb_table, hgrn_out_norm, hgrn_w_out, sc_w_in, sc_conv,
          sc_w_out, ffn_w_up, ffn_conv, ffn_w_down, final_norm, identity, level_masks, out):
    with ExitStack() as ctx:
        def sb(name, shape, dt=F32):
            return ctx.enter_context(nc.sbuf_tensor(name, shape, dt))

        def sem(name):
            return ctx.enter_context(nc.semaphore(name))

        with nc.sbuf_tensor("act", [P, FT, 2, T], F32R) as act:
            pass
        act_low = sb("act_low", [P, DT, 2, T], F32R)
        scratch_at = ExitStack()

        def scratch(name, shape, dt=F32):
            return scratch_at.enter_context(nc.sbuf_tensor(name, shape, dt))

        fpre = scratch("fpre", [P, TG, T])
        suf = scratch("suf", [P, TG, T])
        qh = scratch("qh", [P, TG, T])
        kh = scratch("kh", [P, TG, T])
        ql = scratch("ql", [P, 2, TG, P])
        kl = scratch("kl", [P, 2, TG, T])
        vh = scratch("vh", [P, TG, T])
        vt = scratch("vt", [P, TG, 2, P])
        a_diag = scratch("a_diag", [P, TG, 2, P])
        a_off = scratch("a_off", [P, TG, P])
        o_sb = scratch("o_sb", [P, TG, T])
        scratch_at.close()
        x_tok = scratch("x_tok", [P, T // P, D])
        rows = scratch("rows", [P, 7, P])
        masks_f32 = scratch("masks_f32", [P, MASKS])
        scratch_at.close()
        act_high = sb("act_high", [P, FT - DT, 2, T], F32R)

        h = sb("h", [P, DT, T])
        xn = sb("xn", [P, DT, 2, T], F32R)
        raw = sb("raw", [P, RING, KC, GC])
        w_hi = sb("w_hi", [P, RING, KC, GC], F32R)
        w_lo = sb("w_lo", [P, RING, KC, GC], F32R)
        pad = sb("pad", [P, TG, T + TAPS - 1])
        ta = sb("ta", [P, TG, T])
        tb = sb("tb", [P, TG, T])
        sq_acc = sb("sq_acc", [P, 2, T])
        std = sb("std", [P, T])
        rs = sb("rs", [P, T])
        par = sb("par", [P, PARS])
        lb = sb("lb", [P, HEADS])
        one_less_lb = sb("one_less_lb", [P, HEADS])
        lb_max = sb("lb_max", [P, HEADS])
        lb_exp = sb("lb_exp", [P, 3, HEADS])
        ident = sb("ident", [P, P])
        ones = sb("ones", [P, P])
        masks = sb("masks", [P, MASKS], U8)

        acc = ctx.enter_context(nc.psum_tensor("acc", [P, SETS, TG, T], F32))
        side = ctx.enter_context(nc.psum_tensor("side", [P, STAGES, TG * T], F32))

        w_loaded = [sem(f"w_loaded{n}") for n in range(RING)]
        loads_begun = sem("loads_begun")
        x_loaded = [sem(f"x_loaded{n}") for n in range(DT // TG)]
        rows_loaded, const_loaded = sem("rows_loaded"), sem("const_loaded")
        hi_ready = sem("hi_ready")
        lo_ready = sem("lo_ready")
        chunk_used = sem("chunk_used")
        acc_free = sem("acc_free")
        stage_done = sem("stage_done")
        stage_free = sem("stage_free")
        inits = sem("inits")
        chain = sem("chain")
        late_chain = sem("late_chain")
        rs_chain = sem("rs_chain")
        par_ready = sem("par_ready")
        masks_ready = sem("masks_ready")
        lb_max_ready, lb_exp_ready = sem("lb_max_ready"), sem("lb_exp_ready")
        h_ready = sem("h_ready")
        sq_ready = sem("sq_ready")
        sq_sum = sem("sq_sum")
        xhi_ready = sem("xhi_ready")
        xn_ready = sem("xn_ready")
        act_ready = sem("act_ready")
        var_ready, std_ready = sem("var_ready"), sem("std_ready")
        gate_in, gate_sig = sem("gate_in"), sem("gate_sig")
        conv_ready, silu_ready = sem("conv_ready"), sem("silu_ready")
        qk_ready = sem("qk_ready")
        v_ready, a_ready = sem("v_ready"), sem("a_ready")
        o_ready = sem("o_ready")
        y_ready, y_tok_ready = sem("y_ready"), sem("y_tok_ready")
        y_turned, y_stored = sem("y_turned"), sem("y_stored")

        block = ctx.enter_context(nc.Block())

        def at(i, per, first):
            return i * per + first

        def rows_of(w, kk, col):
            return w[kk * KC * P:(kk + 1) * KC * P, bass.ds(col, GC)].rearrange("(k p) n -> p k n", p=P)

        @block.sync
        def _(sp):
            def stream(phase, w, column):
                def body(i, first):
                    for g in range(phase.groups):
                        for kk in range(phase.cpg):
                            c = phase.c0 + g * phase.cpg + kk
                            sp.wait_ge(lo_ready, at(i, phase.cpi, c + 1))
                            sp.sem_inc(loads_begun, 1)
                            sp.dma_start(raw[:, c % RING], rows_of(w, kk, column(i, g))) \
                                .then_inc(w_loaded[c % RING], 16)
                with sp.Fori(0, phase.n) as i:
                    body(i, False)

            for g in range(DT // TG):
                sp.dma_start(x_tok[:, :, g * GC:(g + 1) * GC],
                             x[0, :, g * GC:(g + 1) * GC].rearrange("(b p) n -> p b n", p=P)).then_inc(x_loaded[g], 16)
            stream(HGRN_IN, hgrn_w_in[0], lambda i, g: i * GC + [D, 0, 2 * D, 3 * D][g])
            stream(HGRN_OUT, hgrn_w_out[0], lambda i, g: i * (2 * GC) + g * GC)
            stream(UP0, ffn_w_up[0], lambda i, g: i * GC + g * FF)
            stream(DOWN0, ffn_w_down[0], lambda i, g: i * (2 * GC) + g * GC)
            stream(SC_IN, sc_w_in[0], lambda i, g: i * (2 * GC) + (g // 3) * GC + [D, 2 * D, 0][g % 3])
            stream(SC_OUT, sc_w_out[0], lambda i, g: i * (2 * GC) + g * GC)
            stream(UP1, ffn_w_up[1], lambda i, g: i * GC + g * FF)
            stream(DOWN1, ffn_w_down[1], lambda i, g: i * (2 * GC) + g * GC)
            y = out[0].rearrange("(b p) n -> p b n", p=P)
            for n in range(DT // TG):
                sp.wait_ge(y_tok_ready, n + 1)
                sp.dma_start(y[:, :, n * GC:(n + 1) * GC], h[:, n * TG:(n + 1) * TG, :].rearrange(
                    "p (b j) t -> p b (j t)", b=T // P)).then_inc(y_stored, 16)
            sp.wait_ge(y_stored, 16 * (DT // TG))

        @block.gpsimd
        def _(pool):
            for t in (ones, sq_acc, pad):
                nc.gpsimd.memset(t[:], 1.0 if t is ones else 0.0).then_inc(inits, 1)
            pool.wait_ge(xn_ready, DT // TG)
            pool.wait_ge(masks_ready, 1)
            for t in (ql, kl, a_diag):
                nc.gpsimd.memset(t[:], 0.0).then_inc(inits, 1)

        @block.scalar
        def _(act_e):
            act_e.dma_start(ident[:], identity).then_inc(const_loaded, 16)
            act_e.dma_start(masks_f32[:], level_masks).then_inc(const_loaded, 16)
            n = 0
            for w, tile in ((norm_mix, 0), (norm_ffn, 0), (hgrn_lb_table, 0), (hgrn_out_norm, 0), (sc_conv, 1)):
                if tile and n == P:
                    n = 0
                a = w.rearrange("a (t p) -> (a t) p", p=P) if len(w.shape) == 2 else \
                    w.rearrange("l a (t p) -> (l a t) p", p=P)
                act_e.dma_start(rows[n:n + a.shape[0], tile, :], a).then_inc(rows_loaded, 16)
                n += a.shape[0]
            act_e.dma_start(rows[n:n + DT, 1, :], final_norm.rearrange("(t p) -> t p", p=P)).then_inc(rows_loaded, 16)
            fc = ffn_conv.rearrange("l a (t p) -> (l a t) p", p=P)
            act_e.dma_start(rows[:, 2:6, :], fc[0:4 * P, :].rearrange("(t p) n -> p t n", p=P)).then_inc(rows_loaded, 16)
            act_e.dma_start(rows[0:FFN_ROWS - 4 * P, 6, :], fc[4 * P:FFN_ROWS, :]).then_inc(rows_loaded, 16)

            def split(i, phase, c):
                act_e.wait_ge(w_loaded[c % RING], at(i, 4 * phase.cpi, 16 * (c // RING + 1)))
                act_e.wait_ge(chunk_used, at(i, phase.cpi, c + 1))
                nc.scalar.activation(w_hi[:, c % RING], raw[:, c % RING], ACT.Copy).then_inc(hi_ready, 1)

            def phase_of(phase, pieces, peel_last=False):
                def body(i, first):
                    for g in range(phase.groups):
                        for kk in range(phase.cpg):
                            c = phase.c0 + g * phase.cpg + kk
                            last = isinstance(i, int) and i * phase.cpi + c + RING >= CHUNKS
                            if not last:
                                split(i, phase, c + RING)
                            pieces(i, first, g, kk)
                loop(act_e, phase, body, peel_last)

            def root(n):
                act_e.wait_ge(var_ready, n + 1)
                nc.scalar.activation(std[:], std[:], ACT.Sqrt).then_inc(std_ready, 1)

            def high_parts(tile, weight):
                for j in range(TG):
                    o = nc.scalar.activation(xn[:, bass.ds(tile + j, 1), 0, :], h[:, bass.ds(tile + j, 1), :],
                                             ACT.Copy, scale=par[:, bass.ds(weight + tile + j, 1)])
                o.then_inc(xhi_ready, 1)

            def residual(i, per, r, tile, weight):
                act_e.wait_ge(h_ready, at(i, per, r + 1))
                nc.scalar.activation(ta[:], h[:, bass.ds(tile, TG), :], ACT.Square).then_inc(sq_ready, 1)
                if weight is not None:
                    high_parts(tile, weight)

            def residual_phase(phase, r0, weight, rs_n=None, peel_last=False):
                def pieces(i, first, g, kk):
                    if rs_n is not None and first and (g, kk) == (0, RING):
                        root(rs_n)
                    if kk == phase.cpg - 1:
                        residual(i, 2, r0 + g, i * (2 * TG) + g * TG, weight)
                phase_of(phase, pieces, peel_last)

            def up_phase(phase, n, rs_n):
                def pieces(i, first, g, kk):
                    if first and (g, kk) == (0, RING):
                        root(rs_n)
                    if (g, kk) == (1, 2):
                        act_e.wait_ge(conv_ready, at(i, 1, n + 1))
                        nc.scalar.activation(ta[:], ta[:], ACT.Silu).then_inc(silu_ready, 1)
                phase_of(phase, pieces)

            act_e.wait_ge(par_ready, 1)
            for g in range(DT // TG):
                act_e.wait_ge(h_ready, g + 1)
                high_parts(g * TG, NORM_MIX)
                split(0, HGRN_IN, g)
            for g in range(DT // TG):
                if g >= 2:
                    act_e.wait_ge(sq_sum, g - 1)
                nc.scalar.activation([ta, tb][g % 2][:], h[:, g * TG:(g + 1) * TG, :], ACT.Square).then_inc(sq_ready, 1)
            act_e.wait_ge(lb_max_ready, 1)
            nc.scalar.activation(lb_exp[:], lb_exp[:], ACT.Exp).then_inc(lb_exp_ready, 1)

            def hgrn(i, first, g, kk):
                if first and (g, kk) == (0, RING):
                    root(0)
                if (g, kk) in ((1, 0), (2, 0), (3, HGRN_IN.cpg - 1)):
                    act_e.wait_ge(gate_in, at(i, 3, {1: 1, 2: 2, 3: 3}[g]))
                    nc.scalar.activation(tb[:], ta[:], ACT.Sigmoid).then_inc(gate_sig, 1)
                if (g, kk) == (3, HGRN_IN.cpg - 1):
                    act_e.wait_ge(o_ready, at(i, 1, 1))
                    nc.scalar.activation(qh[:], o_sb[:], ACT.Square).then_inc(sq_ready, 1)

            phase_of(HGRN_IN, hgrn)
            residual_phase(HGRN_OUT, 4, NORM_FFN, rs_n=1)
            up_phase(UP0, 0, 2)
            residual_phase(DOWN0, 8, NORM_MIX + DT)

            def sc(i, first, g, kk):
                if first and (g, kk) == (0, RING):
                    root(3)
            phase_of(SC_IN, sc)
            residual_phase(SC_OUT, 12, NORM_FFN + DT)
            up_phase(UP1, UP0.n, 4)
            residual_phase(DOWN1, 16, None, peel_last=True)
            act_e.wait_ge(var_ready, 6)
            nc.scalar.activation(std[:, 0:2], std[:, 0:2], ACT.Sqrt).then_inc(std_ready, 1)

        @block.vector
        def _(dve):
            v = nc.vector
            links = [0, 0, 0]

            def link(ins, i):
                links[2] += 1
                ins.then_inc(chain, 1)
                dve.wait_ge(chain, at(i, links[1], links[0] + links[2]))

            def phase_of(phase, pieces, peel_last=False):
                def body(i, first):
                    if links[1] == 0:
                        assert first
                    links[2] = 0
                    for g in range(phase.groups):
                        for kk in range(phase.cpg):
                            c = phase.c0 + g * phase.cpg + kk
                            last = isinstance(i, int) and i * phase.cpi + c + RING >= CHUNKS
                            if not last:
                                split(i, phase, c + RING)
                            pieces(i, first, g, kk)
                    if first:
                        links[1] = links[2]
                    assert links[1] == links[2]
                links[1] = 0
                loop(dve, phase, body, peel_last)
                links[0] += phase.n * links[1]
                links[1] = links[2] = 0

            def split(i, phase, c):
                dve.wait_ge(w_loaded[c % RING], at(i, 4 * phase.cpi, 16 * (c // RING + 1)))
                dve.wait_ge(hi_ready, at(i, phase.cpi, c + 1))
                dve.wait_ge(chunk_used, at(i, phase.cpi, c + 1))
                v.tensor_tensor(w_lo[:, c % RING], raw[:, c % RING], w_hi[:, c % RING].bitcast(F32),
                                ALU.subtract).then_inc(lo_ready, 1)

            steps = [0]

            def then(ins):
                steps[0] += 1
                ins.then_inc(rs_chain, 1)
                dve.wait_ge(rs_chain, steps[0])

            def rms(n, stage):
                dve.wait_ge(stage_done, stage + 1)
                v.memset(sq_acc[:], 0.0)
                v.tensor_scalar(std[:], side[:, stage % STAGES, 0:T], 1.0 / D, EPS, ALU.mult, ALU.add) \
                    .then_inc(var_ready, 1)
                dve.wait_ge(var_ready, n + 1)
                v.sem_inc(stage_free, 1)
                dve.wait_ge(std_ready, n + 1)
                then(v.reciprocal(rs[:], std[:]))

            def scaled(i, phase, g, dst):
                dve.wait_ge(chunk_used, at(i, phase.cpi, phase.c0 + (g + 1) * phase.cpg + RING))
                link(v.tensor_tensor(dst, acc[:, g % SETS], rs[:, None, :].to_broadcast([P, TG, T]), ALU.mult), i)
                v.sem_inc(acc_free, 1)

            def add_squares(i, per, n, src):
                dve.wait_ge(sq_ready, at(i, per, n + 1))
                link(v.tensor_tensor(sq_acc[:], sq_acc[:], src[:, 0:2, :], ALU.add), i)
                v.tensor_tensor(sq_acc[:], sq_acc[:], src[:, 2:4, :], ALU.add).then_inc(sq_sum, 1)

            def low_parts(i, per, r, tile, weight):
                dve.wait_ge(xhi_ready, at(i, per, r + 1))
                for j in range(TG):
                    o = v.scalar_tensor_tensor(out=xn[:, bass.ds(tile + j, 1), 1, :], in0=h[:, bass.ds(tile + j, 1), :],
                                               scalar=par[:, bass.ds(weight + tile + j, 1)],
                                               in1=xn[:, bass.ds(tile + j, 1), 0, :].bitcast(F32),
                                               op0=ALU.mult, op1=ALU.subtract)
                o.then_inc(xn_ready, 1)

            def split_act(i, tile, src):
                dst = act[:, bass.ds(tile, TG), :, :]
                link(v.tensor_copy(dst[:, :, 0, :], src), i)
                v.tensor_tensor(dst[:, :, 1, :], src, dst[:, :, 0, :].bitcast(F32), ALU.subtract).then_inc(act_ready, 1)

            late = [0, 0]
            carried = []

            def convolve(link, dst, column, step, tiles=range(TG)):
                for tap in reversed(range(TAPS)):
                    for j in tiles:
                        w = par[:, bass.ds(column + tap * step + j, 1)]
                        src = pad[:, j, tap:tap + T]
                        if tap == TAPS - 1:
                            o = v.tensor_scalar(dst[:, j, :], src, w, None, ALU.mult)
                        else:
                            o = v.scalar_tensor_tensor(out=dst[:, j, :], in0=src, scalar=w, in1=dst[:, j, :],
                                                       op0=ALU.mult, op1=ALU.add)
                    if tap:
                        link(o)
                return o

            def residual_phase(phase, r0, sq0, weight, rs_n=None, rs_stage=None, final=False):
                carry = carried.pop() if carried else None

                def pieces(i, first, g, kk):
                    if rs_n is not None and first and (g, kk) == (0, RING):
                        rms(rs_n, rs_stage)
                    if carry and first:
                        carry(g, kk)
                    if final and kk == RING + 2 and i * 2 + g:
                        n = i * 2 + g - 1
                        dve.wait_ge(stage_done, S_Y + n + 1)
                        v.tensor_copy(h[:, n * TG:(n + 1) * TG, :].rearrange("p j t -> p (j t)"),
                                      side[:, (S_Y + n) % STAGES]).then_inc(y_turned, 1)
                        dve.wait_ge(y_turned, n + 1)
                        v.sem_inc(stage_free, 1)
                    if kk != phase.cpg - 1:
                        return
                    tile = i * (2 * TG) + g * TG
                    dst = h[:, bass.ds(tile, TG), :]
                    if rs_n is not None:
                        scaled(i, phase, g, tb[:])
                        v.tensor_tensor(dst, dst, tb[:], ALU.add).then_inc(h_ready, 1)
                        dve.wait_ge(h_ready, at(i, 2, r0 + g + 1))
                    else:
                        dve.wait_ge(chunk_used, at(i, phase.cpi, phase.c0 + (g + 1) * phase.cpg + RING))
                        v.tensor_tensor(dst, dst, acc[:, g % SETS], ALU.add).then_inc(h_ready, 1)
                        dve.wait_ge(h_ready, at(i, 2, r0 + g + 1))
                        v.sem_inc(acc_free, 1)
                    add_squares(i, 2, sq0 + g, ta)
                    if final:
                        for j in range(TG):
                            o = v.tensor_scalar(h[:, tile + j, :], h[:, tile + j, :], par[:, FINAL + tile + j:FINAL + tile + j + 1],
                                                None, ALU.mult)
                        o.then_inc(y_ready, 1)
                    if weight is not None:
                        low_parts(i, 2, r0 + g, tile, weight)
                phase_of(phase, pieces, final)

            def up_phase(phase, n, rs_n, rs_stage, conv):
                late_links = 7
                late_base = late[0]

                def late_steps(i, g, kk):
                    def late_link(ins):
                        late[1] += 1
                        ins.then_inc(late_chain, 1)
                        dve.wait_ge(late_chain, at(i, late_links, late_base + late[1]))
                    if g or kk > 4:
                        return
                    if kk == 0:
                        late[1] = 0
                        convolve(late_link, tb, conv + FT + i * TG, 2 * FT, (0, 1))
                    elif kk == 1:
                        late_link(convolve(late_link, tb, conv + FT + i * TG, 2 * FT, (2, 3)))
                    elif kk == 2:
                        dve.wait_ge(silu_ready, at(i, 1, n + 1))
                        late_link(v.tensor_tensor(tb[:], ta[:], tb[:], ALU.mult))
                    elif kk == 3:
                        late_link(v.tensor_copy(act[:, bass.ds(i * TG, TG), 0, :], tb[:]))
                    else:
                        dst = act[:, bass.ds(i * TG, TG), :, :]
                        v.tensor_tensor(dst[:, :, 1, :], tb[:], dst[:, :, 0, :].bitcast(F32), ALU.subtract) \
                            .then_inc(act_ready, 1)
                        assert late[1] == late_links

                def pieces(i, first, g, kk):
                    if first and (g, kk) == (0, RING):
                        rms(rs_n, rs_stage)
                    if not first:
                        late_steps(i - 1, g, kk)
                    if kk == phase.cpg - 1:
                        scaled(i, phase, g, pad[:, :, TAPS - 1:])
                    if (g, kk) == (1, 0):
                        convolve(lambda ins: link(ins, i), ta, conv + i * TG, 2 * FT, (0, 1))
                    if (g, kk) == (1, 1):
                        convolve(lambda ins: link(ins, i), ta, conv + i * TG, 2 * FT, (2, 3)).then_inc(conv_ready, 1)
                phase_of(phase, pieces)
                late[0] += late_links * phase.n
                carried.append(lambda g, kk: late_steps(phase.n - 1, g, kk))

            v.sem_inc(lo_ready, RING)
            v.sem_inc(acc_free, SETS)
            v.sem_inc(stage_free, STAGES)
            dve.wait_ge(stage_done, S_PAR + 1)
            v.tensor_copy(par[:, 0:SC_CONV], side[:, S_PAR % STAGES, 0:P])
            v.tensor_copy(par[:, SC_CONV:FFN_CONV], side[:, S_PAR % STAGES, P:P + 4 * DT])
            v.tensor_copy(par[:, FFN_CONV:PARS], side[:, S_PAR % STAGES, 2 * P:2 * P + FFN_ROWS]).then_inc(par_ready, 1)
            dve.wait_ge(par_ready, 1)
            v.sem_inc(stage_free, 1)
            dve.wait_ge(inits, 3)
            for g in range(DT // TG):
                dve.wait_ge(stage_done, S_X + g + 1)
                v.tensor_copy(h[:, g * TG:(g + 1) * TG, :],
                              side[:, (S_X + g) % STAGES].rearrange("p (j t) -> p j t", j=TG)).then_inc(h_ready, 1)
                dve.wait_ge(h_ready, g + 1)
                v.sem_inc(stage_free, 1)
                if g:
                    low_parts(0, 0, g - 1, (g - 1) * TG, NORM_MIX)
                    split(0, HGRN_IN, g - 1)
            low_parts(0, 0, g, g * TG, NORM_MIX)
            split(0, HGRN_IN, g)
            for g in range(DT // TG):
                dve.wait_ge(sq_ready, g + 1)
                src = [ta, tb][g % 2]
                then(v.tensor_tensor(sq_acc[:], sq_acc[:], src[:, 0:2, :], ALU.add))
                v.tensor_tensor(sq_acc[:], sq_acc[:], src[:, 2:4, :], ALU.add).then_inc(sq_sum, 1)
                dve.wait_ge(sq_sum, g + 1)

            table = par[:, LB:LB + 3 * HEADS].rearrange("p (r h) -> p r h", r=3)
            then(v.tensor_tensor(lb_max[:], table[:, 0], table[:, 1], ALU.max))
            then(v.tensor_tensor(lb_max[:], lb_max[:], table[:, 2], ALU.max))
            v.tensor_tensor(lb_exp[:], table, lb_max[:, None, :].to_broadcast([P, 3, HEADS]), ALU.subtract) \
                .then_inc(lb_max_ready, 1)
            dve.wait_ge(lb_exp_ready, 1)
            then(v.tensor_tensor(lb_max[:], lb_exp[:, 0], lb_exp[:, 1], ALU.add))
            then(v.tensor_tensor(lb_max[:], lb_max[:], lb_exp[:, 2], ALU.add))
            then(v.reciprocal(lb_max[:], lb_max[:]))
            then(v.tensor_tensor(lb[:], lb_exp[:, 0], lb_max[:], ALU.mult))
            then(v.tensor_scalar(one_less_lb[:], lb[:], -1.0, 1.0, ALU.mult, ALU.add))

            dve.wait_ge(const_loaded, 32)
            v.tensor_copy(masks[:], masks_f32[:]).then_inc(masks_ready, 1)
            dve.wait_ge(inits, 6)

            last = HGRN_IN.cpg - 1

            def halves(t, n):
                return t.rearrange("p j (b z n) -> p (j b) z n", z=2, n=n)

            def level_operands(i, m):
                n = LEVELS[m]
                pre, su = halves(fpre[:], n), halves(suf[:], n)
                buf = m % 2
                q_to = ql[:, buf].rearrange("p j (w n) -> p (j w) n", n=n)
                if n == 1:
                    v.tensor_tensor(q_to, halves(qh[:], n)[:, :, 1], pre[:, :, 1], ALU.mult) \
                        .then_inc(qk_ready, 1)
                    v.memset(su[:, :, 1], 1.0)
                    link(v.tensor_copy(su[:, :, 0], pre[:, :, 1]), i)
                else:
                    v.tensor_tensor(q_to, halves(qh[:], n)[:, :, 1], pre[:, :, 1], ALU.mult)
                    v.tensor_tensor(halves(kl[:, buf], n)[:, :, 0], halves(kh[:], n)[:, :, 0], su[:, :, 0], ALU.mult) \
                        .then_inc(qk_ready, 1)
                    if m == len(LEVELS) - 1:
                        return
                    shape = [P, TG * T // (2 * n), n]
                    link(v.tensor_tensor(su[:, :, 0], su[:, :, 0], pre[:, :, 1, n - 1:n].to_broadcast(shape),
                                         ALU.mult), i)
                shape = [P, TG * T // (2 * n), n]
                link(v.tensor_tensor(pre[:, :, 1], pre[:, :, 1], pre[:, :, 0, n - 1:n].to_broadcast(shape), ALU.mult), i)

            def take_stage(i, j):
                s = S_HGRN + j
                src = side[:, s % STAGES]
                if j == 11:
                    dve.wait_ge(stage_done, at(i, HGRN_STAGES, s + 1))
                if j == 0:
                    mask = masks[:, None, 0:P].to_broadcast([P, 2 * TG, P])
                    o = v.copy_predicated(a_diag[:].rearrange("p j b t -> p (j b) t"), mask,
                                          src.rearrange("p (m t) -> p m t", t=P))
                elif j < 8:
                    n = LEVELS[j - 1]
                    at_mask = P + (j - 1) * HALF
                    mask = masks[:, at_mask:at_mask + HALF].rearrange("p (w n) -> p w n", n=n)
                    o = v.copy_predicated(
                        a_diag[:].rearrange("p j b (w z n) -> p (j b) w z n", z=2, n=n)[:, :, :, 1],
                        mask[:, None].to_broadcast([P, 2 * TG, HALF // n, n]),
                        src[:, 0:2 * TG * HALF].rearrange("p (m w n) -> p m w n", m=2 * TG, n=n))
                elif j == 8:
                    o = v.tensor_copy(a_off[:], src[:, 0:TG * P].rearrange("p (j t) -> p j t", j=TG))
                elif j < 11:
                    c = 2 * (j - 9)
                    o = v.tensor_copy(vt[:, c:c + 2], src[:, 0:4 * P].rearrange("p (j b d) -> p j b d", j=2, b=2))
                else:
                    o = v.tensor_copy(o_sb[:], src.rearrange("p (j t) -> p j t", j=TG))
                link(o, i)
                v.sem_inc(stage_free, 1)
                if j in (8, 10):
                    v.sem_inc(a_ready, 1)
                if j == 11:
                    v.sem_inc(o_ready, 1)

            def hgrn(i, first, g, kk):
                n = g * HGRN_IN.cpg + kk - 2 * HGRN_IN.cpg
                if first and (g, kk) == (0, RING):
                    rms(0, S_RS_HGRN)
                if kk == last and g in (0, 1, 3):
                    scaled(i, HGRN_IN, g, ta[:])
                    v.sem_inc(gate_in, 1)
                if kk == last and g == 2:
                    scaled(i, HGRN_IN, g, vh[:])
                    v.sem_inc(v_ready, 1)
                if (g, kk) == (1, 0):
                    dve.wait_ge(gate_sig, at(i, 3, 1))
                    for j in range(TG):
                        c = bass.ds(i * TG + j, 1)
                        o = v.tensor_scalar(fpre[:, j, :], tb[:, j, :], one_less_lb[:, c], lb[:, c], ALU.mult, ALU.add)
                    link(o, i)
                    v.tensor_scalar(kh[:], fpre[:], -1.0, 1.0, ALU.mult, ALU.add)
                if n >= 2 and n - 2 <= 10:
                    take_stage(i, n - 2)
                if n == 0:
                    dve.wait_ge(gate_sig, at(i, 3, 2))
                    link(v.scalar_tensor_tensor(out=qh[:], in0=ta[:], scalar=float(P) ** -0.5, in1=tb[:],
                                                op0=ALU.mult, op1=ALU.mult), i)
                    v.sem_inc(qk_ready, 1)
                if 1 <= n <= len(LEVELS):
                    level_operands(i, n - 1)
                if (g, kk) == (3, last):
                    take_stage(i, 11)
                    dve.wait_ge(gate_sig, at(i, 3, 3))
                    link(v.tensor_tensor(tb[:], ta[:], tb[:], ALU.mult), i)
                    for j in range(TG):
                        o = v.scalar_tensor_tensor(out=tb[:, j, :], in0=o_sb[:, j, :],
                                                   scalar=par[:, bass.ds(OUT_NORM + i * TG + j, 1)], in1=tb[:, j, :],
                                                   op0=ALU.mult, op1=ALU.mult)
                    link(o, i)
                    split_act(i, i * TG, tb[:])
                    add_squares(i, 1, 4, qh)

            phase_of(HGRN_IN, hgrn)
            residual_phase(HGRN_OUT, 4, 8, NORM_FFN, 1, S_RS_OUT)
            up_phase(UP0, 0, 2, S_RS_UP0, FFN_CONV)
            residual_phase(DOWN0, 8, 12, NORM_MIX + DT)

            def sc(i, first, g, kk):
                if first and (g, kk) == (0, RING):
                    rms(3, S_RS_SC)
                if kk != last:
                    return
                tile = i * (2 * TG) + (g // 3) * TG
                if g % 3 == 0:
                    scaled(i, SC_IN, g, ta[:])
                elif g % 3 == 1:
                    u = pad[:, :, TAPS - 1:]
                    scaled(i, SC_IN, g, u)
                    link(v.tensor_tensor(u, u, ta[:], ALU.mult), i)
                    link(convolve(lambda ins: link(ins, i), tb, SC_CONV + tile, DT), i)
                else:
                    scaled(i, SC_IN, g, ta[:])
                    link(v.tensor_tensor(tb[:], ta[:], tb[:], ALU.mult), i)
                    split_act(i, tile, tb[:])

            phase_of(SC_IN, sc)
            residual_phase(SC_OUT, 12, 16, NORM_FFN + DT)
            up_phase(UP1, UP0.n, 4, S_RS_UP1, FFN_CONV + TAPS * 2 * FT)
            residual_phase(DOWN1, 16, 20, None, final=True)

            dve.wait_ge(stage_done, S_RS_END + 1)
            v.tensor_scalar(std[:, 0:2], side[:, S_RS_END % STAGES, 0:2], 1.0 / D, EPS, ALU.mult, ALU.add) \
                .then_inc(var_ready, 1)
            dve.wait_ge(var_ready, 6)
            v.sem_inc(stage_free, 1)
            dve.wait_ge(std_ready, 6)
            then(v.reciprocal(rs[:, 0:2], std[:, 0:2]))
            for n in range(DT // TG):
                y = h[:, n * TG:(n + 1) * TG, :].rearrange("p (b j) t -> p b (j t)", b=T // P)
                src = y
                if n == DT // TG - 1:
                    dve.wait_ge(stage_done, S_Y + n + 1)
                    src = side[:, (S_Y + n) % STAGES].rearrange("p (b n) -> p b n", b=T // P)
                for b in range(T // P):
                    o = v.tensor_scalar(y[:, b], src[:, b], rs[:, b:b + 1], None, ALU.mult)
                o.then_inc(y_tok_ready, 1)

        @block.tensor
        def _(pe):
            mm = nc.tensor.matmul

            def stage(s, steps, i=0, per=0):
                pe.wait_ge(stage_free, at(i, per, s + 1))
                for step in steps:
                    o = step(side[:, s % STAGES])
                o.then_inc(stage_done, 1)

            def turn(src, column, n=P):
                return lambda to: nc.tensor.transpose(to[:, column:column + n], src, ident[0:n, 0:n])

            def sum_squares(n, s):
                pe.wait_ge(sq_sum, DT // TG * (n + 1))
                stage(s, [lambda to, j=j: mm(to[:, 0:T], ones[:], sq_acc[:, j, :], start=(j == 0), stop=(j == 1))
                          for j in range(2)])

            def phase_of(phase, src, ready, ready0, rs=None, pieces=None):
                def body(i, first):
                    for g in range(phase.groups):
                        to = acc[:, g % SETS]
                        for kk in range(phase.cpg):
                            c = phase.c0 + g * phase.cpg + kk
                            if kk == 0:
                                pe.wait_ge(acc_free, at(i, phase.groups, phase.g0 + g + 1))
                            if first and g == 0 and kk * KC % TG == 0:
                                pe.wait_ge(ready, ready0 + kk * KC // TG + 1)
                            pe.wait_ge(hi_ready, at(i, phase.cpi, c + 1))
                            pe.wait_ge(lo_ready, at(i, phase.cpi, c + 1 + RING))
                            for k in range(KC):
                                t = kk * KC + k
                                begin, end = t == 0, t == phase.cpg * KC - 1
                                for j in range(TG):
                                    hi, lo = (w[:, c % RING, k, j * P:(j + 1) * P] for w in (w_hi, w_lo))
                                    mm(to[:, j, :], hi, src[:, t, 0, :], start=begin and j % 2 == 0, stop=False,
                                       skip_group_check=True)
                                    mm(to[:, j, :], hi, src[:, t, 1, :], start=False, stop=False, skip_group_check=True)
                                    o = mm(to[:, j, :], lo, src[:, t, 0, :], start=False, stop=end, skip_group_check=True)
                            o.then_inc(chunk_used, 1)
                            if first and rs and (g, kk) == (0, RING):
                                sum_squares(*rs)
                            if pieces:
                                pieces(i, g, kk)
                loop(pe, phase, body)

            pe.sem_inc(chunk_used, RING)
            pe.wait_ge(const_loaded, 32)
            pe.wait_ge(rows_loaded, 16 * 8)
            stage(S_PAR, [turn(rows[:, 0, :], 0), turn(rows[0:4 * DT, 1, :], P, 4 * DT)] +
                  [turn(rows[:, 2 + t, :], (2 + t) * P) for t in range(4)] +
                  [turn(rows[0:FFN_ROWS - 4 * P, 6, :], 6 * P, FFN_ROWS - 4 * P)])
            for g in range(DT // TG):
                pe.wait_ge(x_loaded[g], 16)
                stage(S_X + g, [turn(x_tok[:, b, (g * TG + j) * P:(g * TG + j + 1) * P], j * T + b * P)
                                for j in range(TG) for b in range(T // P)])
            pe.wait_ge(inits, 3)

            def hgrn(i, g, kk):
                n = g * HGRN_IN.cpg + kk - 2 * HGRN_IN.cpg
                s = S_HGRN + n - 1
                if 1 <= n <= 9:
                    m = n - 2
                    lhs = kh[:] if m < 1 else kl[:, m % 2]
                    pe.wait_ge(qk_ready, at(i, 9, n))
                    if m < 0:
                        steps = [lambda to, j=j, b=b: mm(to[:, (2 * j + b) * P:(2 * j + b + 1) * P],
                                                         kh[:, j, b * P:(b + 1) * P], qh[:, j, b * P:(b + 1) * P],
                                                         start=True, stop=True)
                                 for j in range(TG) for b in range(2)]
                    elif m < len(LEVELS) - 1:
                        steps = [lambda to, j=j, b=b: mm(to[:, (2 * j + b) * HALF:(2 * j + b + 1) * HALF],
                                                         lhs[:, j, b * P:(b + 1) * P],
                                                         ql[:, m % 2, j, b * HALF:(b + 1) * HALF],
                                                         start=True, stop=True)
                                 for j in range(TG) for b in range(2)]
                    else:
                        steps = [lambda to, j=j: mm(to[:, j * P:(j + 1) * P], lhs[:, j, 0:P], ql[:, m % 2, j, :],
                                                    start=True, stop=True) for j in range(TG)]
                    stage(s, steps, i, HGRN_STAGES)
                elif n in (10, 11):
                    if n == 10:
                        pe.wait_ge(v_ready, at(i, 1, 1))
                    j0 = 2 * (n - 10)
                    stage(s, [turn(vh[:, j0 + j, b * P:(b + 1) * P], (2 * j + b) * P) for j in range(2) for b in range(2)],
                          i, HGRN_STAGES)
                elif (g, kk) == (3, HGRN_IN.cpg - 1):
                    pe.wait_ge(a_ready, at(i, 2, 2))
                    steps = []
                    for j in range(TG):
                        for b, a, col, begin, end in ((0, a_diag[:, j, 0], 0, j % 2 == 0, True),
                                                      (0, a_off[:, j], P, False, False),
                                                      (1, a_diag[:, j, 1], P, False, True)):
                            steps.append(lambda to, j=j, b=b, a=a, col=col, begin=begin, end=end: mm(
                                to[:, j * T + col:j * T + col + P], vt[:, j, b], a, start=begin, stop=end,
                                skip_group_check=True))
                    stage(S_HGRN + 11, steps, i, HGRN_STAGES)

            G = DT // TG
            phase_of(HGRN_IN, xn, xn_ready, 0, (0, S_RS_HGRN), hgrn)
            phase_of(HGRN_OUT, act, act_ready, 0, (1, S_RS_OUT))
            phase_of(UP0, xn, xn_ready, G, (2, S_RS_UP0))
            phase_of(DOWN0, act, act_ready, G)
            phase_of(SC_IN, xn, xn_ready, 2 * G, (3, S_RS_SC))
            phase_of(SC_OUT, act, act_ready, G + UP0.n)
            phase_of(UP1, xn, xn_ready, 3 * G, (4, S_RS_UP1))

            def turn_y(n):
                pe.wait_ge(y_ready, n + 1)
                stage(S_Y + n, [turn(h[:, n * TG + j, b * P:(b + 1) * P], (b * TG + j) * P)
                                for b in range(T // P) for j in range(TG)])

            def turn_before(i, g, kk):
                if kk == RING and i * 2 + g:
                    turn_y(i * 2 + g - 1)

            phase_of(DOWN1, act, act_ready, 2 * G + UP0.n, pieces=turn_before)
            pe.wait_ge(y_ready, G)
            turn_y(G - 1)
            pe.wait_ge(sq_sum, G * 6)
            stage(S_RS_END, [lambda to, b=b, j=j: mm(to[:, b:b + 1], sq_acc[:, j, b * P:(b + 1) * P], ones[:, 0:1],
                                                     start=(j == 0), stop=(j == 1))
                             for b in range(T // P) for j in range(2)])


_INS = ["x", "norm_mix", "norm_ffn", "hgrn_w_in", "hgrn_lb_table", "hgrn_out_norm", "hgrn_w_out", "sc_w_in",
        "sc_conv", "sc_w_out", "ffn_w_up", "ffn_conv", "ffn_w_down", "final_norm"]


def kernel(**inputs):
    import numpy as np
    import concourse.bacc as bacc
    from concourse.bass_utils import run_bass_kernel_spmd

    nc = bacc.Bacc("TRN2", target_bir_lowering=False, num_devices=1)
    arrays = {f"in_{name}": np.ascontiguousarray(inputs[name]) for name in _INS}
    s, t = np.arange(P)[:, None], np.arange(P)[None, :]
    pairs = [((s // (2 * n) == t // (2 * n)) & (s // n % 2 == 0))[:, np.arange(P) // n % 2 == 1] for n in LEVELS[:-1]]
    arrays["in_identity"] = np.eye(P, dtype=np.float32)
    arrays["in_level_masks"] = np.concatenate([s == t] + pairs, axis=1).astype(np.float32)
    args = [nc.dram_tensor(k, a.shape, mybir.dt.from_np(a.dtype), kind="ExternalInput").ap() for k, a in arrays.items()]
    args.append(nc.dram_tensor("out", (1, T, D), F32, kind="ExternalOutput").ap())
    trunk(nc, *args)
    return run_bass_kernel_spmd(nc, [arrays], core_ids=[0]).results[0]["out"]
```

```python
from contextlib import ExitStack

import concourse.bass as bass
from concourse import mybir

F32 = mybir.dt.float32
F32R = mybir.dt.float32r
U8 = mybir.dt.uint8
ALU = mybir.AluOpType
ACT = mybir.ActivationFunctionType

P = 128
D = 2048
T = 256
FF = 5632
TAPS = 3
EPS = 1e-6
DT = D // P
FT = FF // P
HEADS = 16
TG = 4
GC = TG * P
KC = 2
RING = 4
STAGES = 2
SETS = 2
LEVELS = [1, 2, 4, 8, 16, 32, 64, 128]
HALF = P // 2
MASKS = P + (len(LEVELS) - 2) * HALF

NORM_MIX, NORM_FFN, LB, OUT_NORM = 0, 2 * DT, 4 * DT, 7 * DT
SC_CONV = 8 * DT
FINAL = SC_CONV + TAPS * DT
FFN_CONV = FINAL + DT
FFN_ROWS = 2 * TAPS * 2 * FT
PARS = FFN_CONV + FFN_ROWS


class Phase:

    def __init__(self, before, n, groups, k_tiles):
        self.n, self.groups, self.cpg = n, groups, k_tiles // KC
        self.cpi = groups * self.cpg
        self.c0 = before.c0 + before.n * before.cpi if before else 0
        self.g0 = before.g0 + before.n * before.groups if before else 0
        assert self.cpi % RING == 0 and self.c0 % RING == 0 and groups % SETS == 0


HGRN_IN = Phase(None, 4, 4, DT)
HGRN_OUT = Phase(HGRN_IN, 2, 2, DT)
UP0 = Phase(HGRN_OUT, 11, 2, DT)
DOWN0 = Phase(UP0, 2, 2, FT)
SC_IN = Phase(DOWN0, 2, 6, DT)
SC_OUT = Phase(SC_IN, 2, 2, DT)
UP1 = Phase(SC_OUT, 11, 2, DT)
DOWN1 = Phase(UP1, 2, 2, FT)
CHUNKS = DOWN1.c0 + DOWN1.n * DOWN1.cpi

S_X = [0, 2, 3, 4]
S_PAR, S_CONV_PAR = 1, 5
CONV_PAR_AT = 3
X_EARLY = 2
X_LOADED_BEFORE = {1: 1, 3: 2, 4: 3}
X_LATE = {0: 2, 2: 3}
SQUARES_AT = [1, 3, 4, 5]
S_RS_HGRN = S_CONV_PAR + 1
S_HGRN = S_RS_HGRN + 1
LEVEL, OUTPUT = range(2)
PLAN = [(2, LEVEL, -1), (3, LEVEL, 0), (5, LEVEL, 1), (6, LEVEL, 2), (8, LEVEL, 3), (10, LEVEL, 4),
        (12, LEVEL, 5), (13, LEVEL, 6), (15, LEVEL, 7), (18, OUTPUT, 0)]
V_GROUP = 2
LEAD = 2
HGRN_STAGES = len(PLAN)
RS_AT = 6
LATE_RS_AT = 8
S_RS_OUT = S_HGRN + HGRN_STAGES * HGRN_IN.n
S_RS_UP0, S_RS_SC, S_RS_UP1, S_Y = (S_RS_OUT + n for n in (1, 2, 3, 4))
S_RS_END = S_Y + DT // TG


def loop(e, phase, body, peel_last=False):
    body(0, True)
    end = phase.n - peel_last
    if end > 2:
        with e.Fori(1, end) as i:
            body(i, False)
    elif end == 2:
        body(1, False)
    if peel_last:
        body(phase.n - 1, False)


def trunk(nc, x, norm_mix, norm_ffn, hgrn_w_in, hgrn_lb_table, hgrn_out_norm, hgrn_w_out, sc_w_in, sc_conv,
          sc_w_out, ffn_w_up, ffn_conv, ffn_w_down, final_norm, identity, level_masks, out):
    with ExitStack() as ctx:
        def sb(name, shape, dt=F32):
            return ctx.enter_context(nc.sbuf_tensor(name, shape, dt))

        def sem(name):
            return ctx.enter_context(nc.semaphore(name))

        with nc.sbuf_tensor("act", [P, FT, 2, T], F32R) as act:
            pass
        act_low = sb("act_low", [P, DT, 2, T], F32R)
        scratch_at = ExitStack()

        def scratch(name, shape, dt=F32):
            return scratch_at.enter_context(nc.sbuf_tensor(name, shape, dt))

        fpre = scratch("fpre", [P, TG, T])
        suf = scratch("suf", [P, TG, T])
        qh = scratch("qh", [P, TG, T])
        kh = scratch("kh", [P, TG, T])
        ql = scratch("ql", [P, 2, TG, P])
        kl = scratch("kl", [P, 2, TG, T])
        vt = scratch("vt", [P, TG, 2, P])
        a_diag = scratch("a_diag", [P, TG, 2, P])
        a_off = scratch("a_off", [P, TG, P])
        o_sb = scratch("o_sb", [P, TG, T])
        scratch_at.close()
        x_tok = scratch("x_tok", [P, T // P, D])
        rows = scratch("rows", [P, 7, P])
        masks_f32 = scratch("masks_f32", [P, MASKS])
        scratch_at.close()
        act_high = sb("act_high", [P, FT - DT, 2, T], F32R)

        h = sb("h", [P, DT, T])
        xn = sb("xn", [P, DT, 2, T], F32R)
        raw = sb("raw", [P, RING, KC, GC])
        w_hi = sb("w_hi", [P, RING, KC, GC], F32R)
        w_lo = sb("w_lo", [P, RING, KC, GC], F32R)
        pad = sb("pad", [P, TG, T + TAPS - 1])
        ta = sb("ta", [P, TG, T])
        tb = sb("tb", [P, TG, T])
        sq_acc = sb("sq_acc", [P, 2, T])
        std = sb("std", [P, T + 2])
        rs = sb("rs", [P, T + 2])
        par = sb("par", [P, PARS])
        lb = sb("lb", [P, HEADS])
        one_less_lb = sb("one_less_lb", [P, HEADS])
        lb_max = sb("lb_max", [P, HEADS])
        lb_exp = sb("lb_exp", [P, 3, HEADS])
        ident = sb("ident", [P, P])
        ones = sb("ones", [P, P])
        masks = sb("masks", [P, MASKS], U8)

        acc = ctx.enter_context(nc.psum_tensor("acc", [P, SETS, TG, T], F32))
        side = ctx.enter_context(nc.psum_tensor("side", [P, STAGES, TG * T], F32))

        w_loaded = [sem(f"w_loaded{n}") for n in range(RING)]
        loads_begun = sem("loads_begun")
        x_loaded = [sem(f"x_loaded{n}") for n in range(DT // TG)]
        rows_loaded, conv_rows_loaded = sem("rows_loaded"), sem("conv_rows_loaded")
        ident_loaded, masks_loaded = sem("ident_loaded"), sem("masks_loaded")
        hi_ready = sem("hi_ready")
        lo_ready = sem("lo_ready")
        chunk_used = sem("chunk_used")
        acc_free = sem("acc_free")
        stage_done = sem("stage_done")
        stage_free = sem("stage_free")
        inits = sem("inits")
        chain = sem("chain")
        late_chain = sem("late_chain")
        once_chain = sem("once_chain")
        par_ready = sem("par_ready")
        masks_ready = sem("masks_ready")
        lb_max_ready = sem("lb_max_ready")
        lb_exp_ready = sem("lb_exp_ready")
        h_ready = sem("h_ready")
        sq_ready = sem("sq_ready")
        sq_sum = sem("sq_sum")
        xhi_ready = sem("xhi_ready")
        xn_ready = sem("xn_ready")
        act_ready = sem("act_ready")
        var_ready = sem("var_ready")
        std_ready = sem("std_ready")
        gate_sig = sem("gate_sig")
        conv_ready = sem("conv_ready")
        silu_ready = sem("silu_ready")
        qk_ready = sem("qk_ready")
        y_ready = sem("y_ready")
        y_turned = sem("y_turned")
        y_scale = sem("y_scale")
        y_tok_ready = sem("y_tok_ready")
        y_scaled = sem("y_scaled")
        y_stored = sem("y_stored")

        block = ctx.enter_context(nc.Block())

        def at(i, per, first):
            return i * per + first

        def rows_of(w, kk, col):
            return w[kk * KC * P:(kk + 1) * KC * P, bass.ds(col, GC)].rearrange("(k p) n -> p k n", p=P)

        @block.sync
        def _(sp):
            def stream(phase, w, column):
                def body(i, first):
                    for g in range(phase.groups):
                        for kk in range(phase.cpg):
                            c = phase.c0 + g * phase.cpg + kk
                            if first and phase is HGRN_IN and g == 0 and kk in X_LOADED_BEFORE:
                                load_x(X_LOADED_BEFORE[kk])
                                if X_LOADED_BEFORE[kk] == DT // TG - 1:
                                    load_late_parameters()
                            sp.wait_ge(lo_ready, at(i, phase.cpi, c + 1))
                            sp.sem_inc(loads_begun, 1)
                            sp.dma_start(raw[:, c % RING], rows_of(w, kk, column(i, g))) \
                                .then_inc(w_loaded[c % RING], 16)
                if phase is HGRN_IN:
                    loop(sp, phase, body)
                else:
                    with sp.Fori(0, phase.n) as i:
                        body(i, False)

            def load_x(g):
                sp.dma_start(x_tok[:, :, g * GC:(g + 1) * GC],
                             x[0, :, g * GC:(g + 1) * GC].rearrange("(b p) n -> p b n", p=P)).then_inc(x_loaded[g], 16)

            def load_late_parameters():
                n = 0
                for w in (sc_conv, final_norm):
                    a = w.rearrange("l a (t p) -> (l a t) p", p=P) if len(w.shape) == 3 else \
                        w.rearrange("(t p) -> t p", p=P)
                    sp.dma_start(rows[n:n + a.shape[0], 1, :], a).then_inc(conv_rows_loaded, 16)
                    n += a.shape[0]
                fc = ffn_conv.rearrange("l a (t p) -> (l a t) p", p=P)
                sp.dma_start(rows[:, 2:6, :], fc[0:4 * P, :].rearrange("(t p) n -> p t n", p=P)) \
                    .then_inc(conv_rows_loaded, 16)
                sp.dma_start(rows[0:FFN_ROWS - 4 * P, 6, :], fc[4 * P:FFN_ROWS, :]).then_inc(conv_rows_loaded, 16)
                sp.dma_start(masks_f32[:], level_masks).then_inc(masks_loaded, 16)

            load_x(0)
            sp.wait_ge(rows_loaded, 16 * 4)
            stream(HGRN_IN, hgrn_w_in[0], lambda i, g: i * GC + [D, 0, 2 * D, 3 * D][g])
            stream(HGRN_OUT, hgrn_w_out[0], lambda i, g: i * (2 * GC) + g * GC)
            stream(UP0, ffn_w_up[0], lambda i, g: i * GC + g * FF)
            stream(DOWN0, ffn_w_down[0], lambda i, g: i * (2 * GC) + g * GC)
            stream(SC_IN, sc_w_in[0], lambda i, g: i * (2 * GC) + (g // 3) * GC + [D, 2 * D, 0][g % 3])
            stream(SC_OUT, sc_w_out[0], lambda i, g: i * (2 * GC) + g * GC)
            stream(UP1, ffn_w_up[1], lambda i, g: i * GC + g * FF)
            stream(DOWN1, ffn_w_down[1], lambda i, g: i * (2 * GC) + g * GC)
            y = out[0].rearrange("(b p) n -> p b n", p=P)
            for n in (2, 0, 3, 1):
                sp.wait_ge(*((y_scaled, n + 1) if n < 2 else (y_tok_ready, n - 1)))
                sp.dma_start(y[:, :, n * GC:(n + 1) * GC], h[:, n * TG:(n + 1) * TG, :].rearrange(
                    "p (b j) t -> p b (j t)", b=T // P)).then_inc(y_stored, 16)
            sp.wait_ge(y_stored, 16 * (DT // TG))

        @block.gpsimd
        def _(pool):
            for t in (ones, sq_acc, pad):
                nc.gpsimd.memset(t[:], 1.0 if t is ones else 0.0).then_inc(inits, 1)
            pool.wait_ge(xn_ready, DT // TG)
            pool.wait_ge(masks_ready, 1)
            for t in (ql, kl, a_diag):
                nc.gpsimd.memset(t[:], 0.0).then_inc(inits, 1)

        @block.scalar
        def _(act_e):
            act_e.dma_start(ident[:], identity).then_inc(ident_loaded, 16)
            n = 0
            for w in (norm_mix, norm_ffn, hgrn_lb_table, hgrn_out_norm):
                a = w.rearrange("a (t p) -> (a t) p", p=P)
                act_e.dma_start(rows[n:n + a.shape[0], 0, :], a).then_inc(rows_loaded, 16)
                n += a.shape[0]

            def split(i, phase, c):
                act_e.wait_ge(w_loaded[c % RING], at(i, 4 * phase.cpi, 16 * (c // RING + 1)))
                act_e.wait_ge(chunk_used, at(i, phase.cpi, c + 1))
                nc.scalar.activation(w_hi[:, c % RING], raw[:, c % RING], ACT.Copy).then_inc(hi_ready, 1)

            def phase_of(phase, pieces, peel_last=False):
                def body(i, first):
                    for g in range(phase.groups):
                        for kk in range(phase.cpg):
                            c = phase.c0 + g * phase.cpg + kk
                            last = isinstance(i, int) and i * phase.cpi + c + RING >= CHUNKS
                            if not last:
                                split(i, phase, c + RING)
                            pieces(i, first, g, kk)
                loop(act_e, phase, body, peel_last)

            def take_x(g):
                act_e.wait_ge(stage_done, S_X[g] + 1)
                nc.scalar.activation(h[:, g * TG:(g + 1) * TG, :],
                                     side[:, S_X[g] % STAGES].rearrange("p (j t) -> p j t", j=TG), ACT.Copy) \
                    .then_inc(h_ready, 1)
                act_e.wait_ge(h_ready, g + 1)

            def root(n, width=T):
                act_e.wait_ge(var_ready, n + 1)
                nc.scalar.activation(std[:, 0:width], std[:, 0:width], ACT.Sqrt).then_inc(std_ready, 1)

            def high_parts(tile, weight):
                for j in range(TG):
                    o = nc.scalar.activation(xn[:, bass.ds(tile + j, 1), 0, :], h[:, bass.ds(tile + j, 1), :],
                                             ACT.Copy, scale=par[:, bass.ds(weight + tile + j, 1)])
                o.then_inc(xhi_ready, 1)

            def residual(i, per, r, tile, weight):
                act_e.wait_ge(h_ready, at(i, per, r + 1))
                nc.scalar.activation(ta[:], h[:, bass.ds(tile, TG), :], ACT.Square).then_inc(sq_ready, 1)
                if weight is not None:
                    high_parts(tile, weight)

            def residual_phase(phase, r0, weight, rs_n=None, peel_last=False, carry=None):
                def pieces(i, first, g, kk):
                    if carry and first:
                        carry(g, kk)
                    if rs_n is not None and first and (g, kk) == (0, RS_AT):
                        root(rs_n)
                    if kk == phase.cpg - 1:
                        residual(i, 2, r0 + g, i * (2 * TG) + g * TG, weight)
                phase_of(phase, pieces, peel_last)

            def up_phase(phase, n, rs_n):
                def pieces(i, first, g, kk):
                    if first and (g, kk) == (0, RS_AT):
                        root(rs_n)
                    if (g, kk) == (1, 2):
                        act_e.wait_ge(conv_ready, at(i, 1, n + 1))
                        nc.scalar.activation(ta[:], ta[:], ACT.Silu).then_inc(silu_ready, 1)
                phase_of(phase, pieces)

            act_e.wait_ge(inits, 1)
            nc.scalar.activation(std[:, 0:1], ones[:, 0:1], ACT.Copy)
            for g in range(X_EARLY):
                take_x(g)
                if g == 0:
                    act_e.wait_ge(par_ready, 1)
                high_parts(g * TG, NORM_MIX)
                split(0, HGRN_IN, 2 * g)
                split(0, HGRN_IN, 2 * g + 1)
                if g == 0:
                    act_e.wait_ge(lb_max_ready, 1)
                    nc.scalar.activation(lb_exp[:], lb_exp[:], ACT.Exp).then_inc(lb_exp_ready, 1)

            def output_steps(i, g, kk):
                if (g, kk) == (0, 0):
                    act_e.wait_ge(acc_free, at(i, HGRN_IN.groups, 4 + SETS))
                    nc.scalar.activation(tb[:], ta[:], ACT.Sigmoid).then_inc(gate_sig, 1)
                if (g, kk) == (0, 3):
                    act_e.wait_ge(stage_free, at(i, HGRN_STAGES, S_HGRN + HGRN_STAGES + STAGES))
                    nc.scalar.activation(qh[:], o_sb[:], ACT.Square).then_inc(sq_ready, 1)

            def hgrn(i, first, g, kk):
                if first and g == 0 and kk in X_LATE:
                    take_x(X_LATE[kk])
                    high_parts(X_LATE[kk] * TG, NORM_MIX)
                if first and g == 0 and kk in SQUARES_AT:
                    n = SQUARES_AT.index(kk)
                    if n >= 2:
                        act_e.wait_ge(sq_sum, n - 1)
                    nc.scalar.activation([ta, tb][n % 2][:], h[:, n * TG:(n + 1) * TG, :], ACT.Square) \
                        .then_inc(sq_ready, 1)
                if first and (g, kk) == (0, HGRN_IN.cpg - 1):
                    root(0, T + 2)
                if (g, kk) in ((1, 0), (2, 0)):
                    act_e.wait_ge(acc_free, at(i, HGRN_IN.groups, g + SETS))
                    nc.scalar.activation(tb[:], ta[:], ACT.Sigmoid).then_inc(gate_sig, 1)
                if not first:
                    output_steps(i - 1, g, kk)

            phase_of(HGRN_IN, hgrn)
            residual_phase(HGRN_OUT, 4, NORM_FFN, rs_n=1, carry=lambda g, kk: output_steps(HGRN_IN.n - 1, g, kk))
            up_phase(UP0, 0, 2)
            residual_phase(DOWN0, 8, NORM_MIX + DT)

            def sc(i, first, g, kk):
                if first and (g, kk) == (0, RS_AT):
                    root(3)
            phase_of(SC_IN, sc)
            residual_phase(SC_OUT, 12, NORM_FFN + DT)
            up_phase(UP1, UP0.n, 4)
            residual_phase(DOWN1, 16, None, peel_last=True)
            act_e.wait_ge(var_ready, 6)
            nc.scalar.activation(std[:, 0:2], std[:, 0:2], ACT.Sqrt).then_inc(std_ready, 1)
            act_e.wait_ge(y_scale, 1)
            act_e.wait_ge(y_turned, DT // TG - 1)
            for n in range(2):
                y = h[:, n * TG:(n + 1) * TG, :].rearrange("p (b j) t -> p b (j t)", b=T // P)
                for b in range(T // P):
                    o = nc.scalar.activation(y[:, b], y[:, b], ACT.Copy, scale=rs[:, b:b + 1])
                o.then_inc(y_scaled, 1)

        @block.vector
        def _(dve):
            v = nc.vector
            links = [0, 0, 0]

            def link(ins, i):
                links[2] += 1
                ins.then_inc(chain, 1)
                dve.wait_ge(chain, at(i, links[1], links[0] + links[2]))

            def mark(ins):
                links[2] += 1
                return ins.then_inc(chain, 1)

            def await_mark(i):
                dve.wait_ge(chain, at(i, links[1], links[0] + links[2]))

            def phase_of(phase, pieces, peel_last=False, ahead=None):
                def body(i, first):
                    links[2] = 0
                    for g in range(phase.groups):
                        for kk in range(phase.cpg):
                            c = phase.c0 + g * phase.cpg + kk
                            last = isinstance(i, int) and i * phase.cpi + c + RING >= CHUNKS
                            if ahead:
                                ahead(i, g, kk)
                            if not last:
                                split(i, phase, c + RING)
                            pieces(i, first, g, kk)
                    if first:
                        links[1] = links[2]
                    assert links[1] == links[2]
                links[1] = 0
                loop(dve, phase, body, peel_last)
                links[0] += phase.n * links[1]
                links[1] = links[2] = 0

            def split(i, phase, c):
                dve.wait_ge(hi_ready, at(i, phase.cpi, c + 1))
                v.tensor_tensor(w_lo[:, c % RING], raw[:, c % RING], w_hi[:, c % RING].bitcast(F32),
                                ALU.subtract).then_inc(lo_ready, 1)

            once_steps = [0]

            def then(ins):
                once_steps[0] += 1
                ins.then_inc(once_chain, 1)
                dve.wait_ge(once_chain, once_steps[0])

            def rms(n, stage, width=T):
                dve.wait_ge(stage_done, stage + 1)
                v.memset(sq_acc[:], 0.0)
                v.tensor_scalar(std[:, 0:width], side[:, stage % STAGES, 0:width], 1.0 / D, EPS, ALU.mult, ALU.add) \
                    .then_inc(var_ready, 1)
                dve.wait_ge(var_ready, n + 1)
                v.sem_inc(stage_free, 1)
                dve.wait_ge(std_ready, n + 1)
                then(v.reciprocal(rs[:, 0:width], std[:, 0:width]))

            def scaled(i, phase, g, dst):
                dve.wait_ge(chunk_used, at(i, phase.cpi, phase.c0 + (g + 1) * phase.cpg + RING))
                v.tensor_tensor(dst, acc[:, g % SETS], rs[:, None, 0:T].to_broadcast([P, TG, T]), ALU.mult) \
                    .then_inc(acc_free, 1)

            def await_scaled(i, phase, g):
                dve.wait_ge(acc_free, at(i, phase.groups, phase.g0 + g + 1 + SETS))

            def add_squares(i, per, n, src):
                dve.wait_ge(sq_ready, at(i, per, n + 1))
                link(v.tensor_tensor(sq_acc[:], sq_acc[:], src[:, 0:2, :], ALU.add), i)
                v.tensor_tensor(sq_acc[:], sq_acc[:], src[:, 2:4, :], ALU.add).then_inc(sq_sum, 1)

            def low_parts(i, per, r, tile, weight):
                dve.wait_ge(xhi_ready, at(i, per, r + 1))
                for j in range(TG):
                    o = v.scalar_tensor_tensor(out=xn[:, bass.ds(tile + j, 1), 1, :], in0=h[:, bass.ds(tile + j, 1), :],
                                               scalar=par[:, bass.ds(weight + tile + j, 1)],
                                               in1=xn[:, bass.ds(tile + j, 1), 0, :].bitcast(F32),
                                               op0=ALU.mult, op1=ALU.subtract)
                o.then_inc(xn_ready, 1)

            def split_act(i, tile, src):
                dst = act[:, bass.ds(tile, TG), :, :]
                link(v.tensor_copy(dst[:, :, 0, :], src), i)
                v.tensor_tensor(dst[:, :, 1, :], src, dst[:, :, 0, :].bitcast(F32), ALU.subtract).then_inc(act_ready, 1)

            late = [0, 0]
            carried = []

            def convolve(link, dst, column, step, tiles=range(TG)):
                for tap in reversed(range(TAPS)):
                    for j in tiles:
                        w = par[:, bass.ds(column + tap * step + j, 1)]
                        src = pad[:, j, tap:tap + T]
                        if tap == TAPS - 1:
                            o = v.tensor_scalar(dst[:, j, :], src, w, None, ALU.mult)
                        else:
                            o = v.scalar_tensor_tensor(out=dst[:, j, :], in0=src, scalar=w, in1=dst[:, j, :],
                                                       op0=ALU.mult, op1=ALU.add)
                    if tap:
                        link(o)
                return o

            def residual_phase(phase, r0, sq0, weight, rs_n=None, rs_stage=None, final=False):
                carry = carried.pop() if carried else None

                def pieces(i, first, g, kk):
                    if carry and first:
                        carry(g, kk)
                    if rs_n is not None and first and (g, kk) == (0, RS_AT):
                        rms(rs_n, rs_stage)
                    if final and kk == RING + 2 and i * 2 + g:
                        n = i * 2 + g - 1
                        dve.wait_ge(stage_done, S_Y + n + 1)
                        v.tensor_copy(h[:, n * TG:(n + 1) * TG, :].rearrange("p j t -> p (j t)"),
                                      side[:, (S_Y + n) % STAGES]).then_inc(y_turned, 1)
                        dve.wait_ge(y_turned, n + 1)
                        v.sem_inc(stage_free, 1)
                    if kk != phase.cpg - 1:
                        return
                    tile = i * (2 * TG) + g * TG
                    dst = h[:, bass.ds(tile, TG), :]
                    if rs_n is not None:
                        scaled(i, phase, g, tb[:])
                        await_scaled(i, phase, g)
                        v.tensor_tensor(dst, dst, tb[:], ALU.add).then_inc(h_ready, 1)
                        dve.wait_ge(h_ready, at(i, 2, r0 + g + 1))
                    else:
                        dve.wait_ge(chunk_used, at(i, phase.cpi, phase.c0 + (g + 1) * phase.cpg + RING))
                        v.tensor_tensor(dst, dst, acc[:, g % SETS], ALU.add).then_inc(h_ready, 1)
                        dve.wait_ge(h_ready, at(i, 2, r0 + g + 1))
                        v.sem_inc(acc_free, 1)
                    if final:
                        for j in range(TG):
                            o = v.tensor_scalar(tb[:, j, :], h[:, tile + j, :],
                                                par[:, FINAL + tile + j:FINAL + tile + j + 1], None, ALU.mult)
                        o.then_inc(y_ready, 1)
                    add_squares(i, 2, sq0 + g, ta)
                    if weight is not None:
                        low_parts(i, 2, r0 + g, tile, weight)
                phase_of(phase, pieces, final)

            def up_phase(phase, n, rs_n, rs_stage, conv):
                late_links = 7
                late_base = late[0]

                def late_steps(i, g, kk):
                    def late_link(ins):
                        late[1] += 1
                        ins.then_inc(late_chain, 1)
                        dve.wait_ge(late_chain, at(i, late_links, late_base + late[1]))
                    if g or kk > 4:
                        return
                    if kk == 0:
                        late[1] = 0
                        await_scaled(i, phase, 1)
                        convolve(late_link, tb, conv + FT + i * TG, 2 * FT, (0, 1))
                    elif kk == 1:
                        late_link(convolve(late_link, tb, conv + FT + i * TG, 2 * FT, (2, 3)))
                    elif kk == 2:
                        dve.wait_ge(silu_ready, at(i, 1, n + 1))
                        late_link(v.tensor_tensor(tb[:], ta[:], tb[:], ALU.mult))
                    elif kk == 3:
                        late_link(v.tensor_copy(act[:, bass.ds(i * TG, TG), 0, :], tb[:]))
                    else:
                        dst = act[:, bass.ds(i * TG, TG), :, :]
                        v.tensor_tensor(dst[:, :, 1, :], tb[:], dst[:, :, 0, :].bitcast(F32), ALU.subtract) \
                            .then_inc(act_ready, 1)
                        assert late[1] == late_links

                def pieces(i, first, g, kk):
                    if first and (g, kk) == (0, RS_AT):
                        rms(rs_n, rs_stage)
                    if not first:
                        late_steps(i - 1, g, kk)
                    if kk == phase.cpg - 1:
                        scaled(i, phase, g, pad[:, :, TAPS - 1:])
                    if (g, kk) == (1, 0):
                        await_scaled(i, phase, 0)
                        convolve(lambda ins: link(ins, i), ta, conv + i * TG, 2 * FT, (0, 1))
                    if (g, kk) == (1, 1):
                        convolve(lambda ins: link(ins, i), ta, conv + i * TG, 2 * FT, (2, 3)).then_inc(conv_ready, 1)
                phase_of(phase, pieces)
                late[0] += late_links * phase.n
                carried.append(lambda g, kk: late_steps(phase.n - 1, g, kk))

            def lower_bound():
                table = par[:, LB:LB + 3 * HEADS].rearrange("p (r h) -> p r h", r=3)
                then(v.tensor_tensor(lb_max[:], table[:, 0], table[:, 1], ALU.max))
                then(v.tensor_tensor(lb_max[:], lb_max[:], table[:, 2], ALU.max))
                v.tensor_tensor(lb_exp[:], table, lb_max[:, None, :].to_broadcast([P, 3, HEADS]), ALU.subtract) \
                    .then_inc(lb_max_ready, 1)

            def lower_bound_rest():
                dve.wait_ge(lb_exp_ready, 1)
                then(v.tensor_tensor(lb_max[:], lb_exp[:, 0], lb_exp[:, 1], ALU.add))
                then(v.tensor_tensor(lb_max[:], lb_max[:], lb_exp[:, 2], ALU.add))
                then(v.reciprocal(lb_max[:], lb_max[:]))
                then(v.tensor_tensor(lb[:], lb_exp[:, 0], lb_max[:], ALU.mult))
                then(v.tensor_scalar(one_less_lb[:], lb[:], -1.0, 1.0, ALU.mult, ALU.add))

            v.sem_inc(lo_ready, RING)
            v.sem_inc(acc_free, SETS)
            v.sem_inc(stage_free, STAGES)

            def x_taken(g):
                dve.wait_ge(h_ready, g + 1)
                v.sem_inc(stage_free, 1)

            x_taken(0)
            dve.wait_ge(stage_done, S_PAR + 1)
            v.tensor_copy(par[:, 0:SC_CONV], side[:, S_PAR % STAGES, 0:P]).then_inc(par_ready, 1)
            dve.wait_ge(par_ready, 1)
            v.sem_inc(stage_free, 1)
            lower_bound()
            dve.wait_ge(inits, 3)
            for g in range(X_EARLY):
                if g:
                    x_taken(g)
                low_parts(0, 0, g, g * TG, NORM_MIX)
                split(0, HGRN_IN, 2 * g)
                split(0, HGRN_IN, 2 * g + 1)
                if g == 0:
                    lower_bound_rest()

            last = HGRN_IN.cpg - 1

            def halves(t, n):
                return t.rearrange("p j (b z n) -> p (j b) z n", z=2, n=n)

            def level_operands(i, m):
                n = LEVELS[m]
                await_mark(i)
                pre, su = halves(fpre[:], n), halves(suf[:], n)
                buf = m % 2
                q_to = ql[:, buf].rearrange("p j (w n) -> p (j w) n", n=n)
                if n == 1:
                    v.tensor_tensor(q_to, halves(qh[:], n)[:, :, 1], pre[:, :, 1], ALU.mult) \
                        .then_inc(qk_ready, 1)
                    v.memset(su[:, :, 1], 1.0)
                    mark(v.tensor_copy(su[:, :, 0], pre[:, :, 1]))
                else:
                    v.tensor_tensor(q_to, halves(qh[:], n)[:, :, 1], pre[:, :, 1], ALU.mult)
                    v.tensor_tensor(halves(kl[:, buf], n)[:, :, 0], halves(kh[:], n)[:, :, 0], su[:, :, 0], ALU.mult) \
                        .then_inc(qk_ready, 1)
                    if m == len(LEVELS) - 1:
                        return
                    shape = [P, TG * T // (2 * n), n]
                    mark(v.tensor_tensor(su[:, :, 0], su[:, :, 0], pre[:, :, 1, n - 1:n].to_broadcast(shape),
                                         ALU.mult))

            def prefixes(i, m):
                n = LEVELS[m]
                pre = halves(fpre[:], n)
                shape = [P, TG * T // (2 * n), n]
                await_mark(i)
                mark(v.tensor_tensor(pre[:, :, 1], pre[:, :, 1], pre[:, :, 0, n - 1:n].to_broadcast(shape), ALU.mult))

            def take_stage(i, stage):
                s = S_HGRN + stage
                _, what, m = PLAN[stage]
                src = side[:, s % STAGES]
                if what == OUTPUT:
                    dve.wait_ge(stage_done, at(i, HGRN_STAGES, s + 1))
                if what == OUTPUT:
                    o = v.tensor_copy(o_sb[:], src.rearrange("p (j t) -> p j t", j=TG))
                elif m < 0:
                    mask = masks[:, None, 0:P].to_broadcast([P, 2 * TG, P])
                    o = v.copy_predicated(a_diag[:].rearrange("p j b t -> p (j b) t"), mask,
                                          src.rearrange("p (m t) -> p m t", t=P))
                elif LEVELS[m] == HALF:
                    o = v.tensor_copy(a_diag[0:HALF].rearrange("p j b t -> p (j b) t")[:, :, HALF:],
                                      src[0:HALF, 0:2 * TG * HALF].rearrange("p (m t) -> p m t", t=HALF))
                elif LEVELS[m] < P:
                    n = LEVELS[m]
                    at_mask = P + m * HALF
                    mask = masks[:, at_mask:at_mask + HALF].rearrange("p (w n) -> p w n", n=n)
                    o = v.copy_predicated(
                        a_diag[:].rearrange("p j b (w z n) -> p (j b) w z n", z=2, n=n)[:, :, :, 1],
                        mask[:, None].to_broadcast([P, 2 * TG, HALF // n, n]),
                        src[:, 0:2 * TG * HALF].rearrange("p (m w n) -> p m w n", m=2 * TG, n=n))
                else:
                    o = v.tensor_copy(a_off[:], src[:, 0:TG * P].rearrange("p (j t) -> p j t", j=TG))
                o.then_inc(stage_free, 1)

            def output_steps(i, g, kk):
                late_links = 4

                def late_link(ins):
                    late[1] += 1
                    ins.then_inc(late_chain, 1)
                    dve.wait_ge(late_chain, at(i, late_links, late[1]))
                if g:
                    return
                if kk == 0:
                    late[1] = 0
                    take_stage(i, HGRN_STAGES - 2)
                if kk == 2:
                    dve.wait_ge(gate_sig, at(i, 3, 3))
                    late_link(v.tensor_tensor(tb[:], ta[:], tb[:], ALU.mult))
                    take_stage(i, HGRN_STAGES - 1)
                    dve.wait_ge(stage_free, at(i, HGRN_STAGES, S_HGRN + HGRN_STAGES + STAGES))
                    for j in range(TG):
                        o = v.scalar_tensor_tensor(out=tb[:, j, :], in0=o_sb[:, j, :],
                                                   scalar=par[:, bass.ds(OUT_NORM + i * TG + j, 1)], in1=tb[:, j, :],
                                                   op0=ALU.mult, op1=ALU.mult)
                    late_link(o)
                if kk == 3:
                    late_link(v.tensor_copy(act[:, bass.ds(i * TG, TG), 0, :], tb[:]))
                    dst = act[:, bass.ds(i * TG, TG), :, :]
                    v.tensor_tensor(dst[:, :, 1, :], tb[:], dst[:, :, 0, :].bitcast(F32), ALU.subtract) \
                        .then_inc(act_ready, 1)
                if kk == 4:
                    dve.wait_ge(sq_ready, at(i, 1, 4 + 1))
                    late_link(v.tensor_tensor(sq_acc[:], sq_acc[:], qh[:, 0:2, :], ALU.add))
                    v.tensor_tensor(sq_acc[:], sq_acc[:], qh[:, 2:4, :], ALU.add).then_inc(sq_sum, 1)
                    assert late[1] == late_links

            def last_take(i, g, kk):
                for stage, (after, what, _) in enumerate(PLAN):
                    if what == LEVEL and g * HGRN_IN.cpg + kk - 2 * HGRN_IN.cpg == after + 2:
                        dve.wait_ge(stage_free, at(i, HGRN_STAGES, S_HGRN + stage + 1 + STAGES))

            def hgrn(i, first, g, kk):
                n = g * HGRN_IN.cpg + kk - 2 * HGRN_IN.cpg
                if first and g == 0 and kk in X_LATE:
                    x_taken(X_LATE[kk])
                    low_parts(0, 0, X_LATE[kk], X_LATE[kk] * TG, NORM_MIX)
                if first and g == 0 and kk in SQUARES_AT:
                    n_sq = SQUARES_AT.index(kk)
                    dve.wait_ge(sq_ready, n_sq + 1)
                    src = [ta, tb][n_sq % 2]
                    then(v.tensor_tensor(sq_acc[:], sq_acc[:], src[:, 0:2, :], ALU.add))
                    then(v.tensor_tensor(sq_acc[:], sq_acc[:], src[:, 2:4, :], ALU.add))
                    v.sem_inc(sq_sum, 1)
                if first and (g, kk) == (0, CONV_PAR_AT):
                    dve.wait_ge(stage_done, S_CONV_PAR + 1)
                    from_psum = side[:, S_CONV_PAR % STAGES]
                    v.tensor_copy(par[:, SC_CONV:FFN_CONV], from_psum[:, 0:4 * DT])
                    v.tensor_copy(par[:, FFN_CONV:PARS], from_psum[:, P:P + FFN_ROWS]).then_inc(par_ready, 1)
                    dve.wait_ge(par_ready, 2)
                    v.sem_inc(stage_free, 1)
                    dve.wait_ge(masks_loaded, 16)
                    v.tensor_copy(masks[:], masks_f32[:]).then_inc(masks_ready, 1)
                if first and (g, kk) == (0, last):
                    rms(0, S_RS_HGRN, T + 2)
                for stage, (after, _, _) in enumerate(PLAN):
                    if n == after + 1:
                        take_stage(i, stage)
                if kk == last and g == V_GROUP:
                    dve.wait_ge(chunk_used, at(i, HGRN_IN.cpi, HGRN_IN.c0 + (g + 1) * HGRN_IN.cpg + RING))
                    for b in range(T // P):
                        o = v.tensor_scalar(vt[:, :, b, :], acc[:, g % SETS, 2 * b:2 * b + 2, :].rearrange(
                            "p a (c d) -> p (a c) d", d=P), rs[:, T + b:T + b + 1], None, ALU.mult)
                    o.then_inc(acc_free, 1)
                elif kk == last:
                    scaled(i, HGRN_IN, g, ta[:])
                if first and (g, kk) == (1, 0):
                    dve.wait_ge(inits, 6)
                if (g, kk) == (1, 0):
                    dve.wait_ge(gate_sig, at(i, 3, 1))
                    for j in range(TG):
                        c = bass.ds(i * TG + j, 1)
                        o = v.tensor_scalar(fpre[:, j, :], tb[:, j, :], one_less_lb[:, c], lb[:, c], ALU.mult, ALU.add)
                    link(o, i)
                    v.tensor_scalar(kh[:], fpre[:], -1.0, 1.0, ALU.mult, ALU.add)
                for after, what, m in PLAN:
                    if what == LEVEL and 0 <= m < len(LEVELS) - 1 and n == after - LEAD + 1:
                        prefixes(i, m)
                if not first:
                    output_steps(i - 1, g, kk)
                if n == 0:
                    dve.wait_ge(gate_sig, at(i, 3, 2))
                    v.scalar_tensor_tensor(out=qh[:], in0=ta[:], scalar=float(P) ** -0.5, in1=tb[:],
                                           op0=ALU.mult, op1=ALU.mult).then_inc(qk_ready, 1)
                    dve.wait_ge(qk_ready, at(i, 1 + len(LEVELS), 1))
                for after, what, m in PLAN:
                    if what == LEVEL and m >= 0 and n == after - LEAD:
                        level_operands(i, m)

            phase_of(HGRN_IN, hgrn, ahead=last_take)
            late[0] += 4 * HGRN_IN.n
            carried.append(lambda g, kk: output_steps(HGRN_IN.n - 1, g, kk))
            residual_phase(HGRN_OUT, 4, 8, NORM_FFN, 1, S_RS_OUT)
            up_phase(UP0, 0, 2, S_RS_UP0, FFN_CONV)
            residual_phase(DOWN0, 8, 12, NORM_MIX + DT)

            def sc(i, first, g, kk):
                if first and (g, kk) == (0, RS_AT):
                    rms(3, S_RS_SC)
                tile = i * (2 * TG) + (g // 3) * TG
                if g % 3 == 2 and kk == 0:
                    link(convolve(lambda ins: link(ins, i), tb, SC_CONV + tile, DT), i)
                if kk != last:
                    return
                if g % 3 == 0:
                    scaled(i, SC_IN, g, ta[:])
                elif g % 3 == 1:
                    u = pad[:, :, TAPS - 1:]
                    scaled(i, SC_IN, g, u)
                    await_scaled(i, SC_IN, g)
                    link(v.tensor_tensor(u, u, ta[:], ALU.mult), i)
                else:
                    scaled(i, SC_IN, g, ta[:])
                    await_scaled(i, SC_IN, g)
                    link(v.tensor_tensor(tb[:], ta[:], tb[:], ALU.mult), i)
                    split_act(i, tile, tb[:])

            phase_of(SC_IN, sc)
            residual_phase(SC_OUT, 12, 16, NORM_FFN + DT)
            up_phase(UP1, UP0.n, 4, S_RS_UP1, FFN_CONV + TAPS * 2 * FT)
            residual_phase(DOWN1, 16, 20, None, final=True)

            dve.wait_ge(stage_done, S_RS_END + 1)
            v.tensor_scalar(std[:, 0:2], side[:, S_RS_END % STAGES, 0:2], 1.0 / D, EPS, ALU.mult, ALU.add) \
                .then_inc(var_ready, 1)
            dve.wait_ge(var_ready, 6)
            v.sem_inc(stage_free, 1)
            dve.wait_ge(std_ready, 6)
            v.reciprocal(rs[:, 0:2], std[:, 0:2]).then_inc(y_scale, 1)
            dve.wait_ge(y_scale, 1)
            for n in range(2, DT // TG):
                y = h[:, n * TG:(n + 1) * TG, :].rearrange("p (b j) t -> p b (j t)", b=T // P)
                src = y
                if n == DT // TG - 1:
                    dve.wait_ge(stage_done, S_Y + n + 1)
                    src = side[:, (S_Y + n) % STAGES].rearrange("p (b n) -> p b n", b=T // P)
                for b in range(T // P):
                    o = v.tensor_scalar(y[:, b], src[:, b], rs[:, b:b + 1], None, ALU.mult)
                o.then_inc(y_tok_ready, 1)

        @block.tensor
        def _(pe):
            mm = nc.tensor.matmul

            def stage(s, steps, i=0, per=0):
                pe.wait_ge(stage_free, at(i, per, s + 1))
                for step in steps:
                    o = step(side[:, s % STAGES])
                o.then_inc(stage_done, 1)

            def turn(src, column, n=P):
                return lambda to: nc.tensor.transpose(to[:, column:column + n], src, ident[0:n, 0:n])

            def token_sums(column):
                return [lambda to, b=b, j=j: mm(to[:, column + b:column + b + 1], sq_acc[:, j, b * P:(b + 1) * P],
                                                ones[:, 0:1], start=(j == 0), stop=(j == 1))
                        for b in range(T // P) for j in range(2)]

            def sum_squares(n, s, tokens_too=False):
                pe.wait_ge(sq_sum, DT // TG * (n + 1))
                stage(s, [lambda to, j=j: mm(to[:, 0:T], ones[:], sq_acc[:, j, :], start=(j == 0), stop=(j == 1))
                          for j in range(2)] + (token_sums(T) if tokens_too else []))

            def phase_of(phase, src, ready, ready0, rs=None, pieces=None, carry=None, rs_at=(0, RS_AT),
                         token_group=None):
                def body(i, first):
                    for g in range(phase.groups):
                        to = acc[:, g % SETS]
                        for kk in range(phase.cpg):
                            c = phase.c0 + g * phase.cpg + kk
                            if kk == 0:
                                pe.wait_ge(acc_free, at(i, phase.groups, phase.g0 + g + 1))
                            if first and g == 0 and kk * KC % TG == 0:
                                pe.wait_ge(ready, ready0 + kk * KC // TG + 1)
                            pe.wait_ge(lo_ready, at(i, phase.cpi, c + 1 + RING))
                            for k in range(KC):
                                t = kk * KC + k
                                begin, end = t == 0, t == phase.cpg * KC - 1
                                if g == token_group:
                                    for b in range(T // P):
                                        bank = to[:, 2 * b:2 * b + 2, :].rearrange("p j t -> p (j t)")
                                        x_hi, x_lo = (src[:, t, n, b * P:(b + 1) * P] for n in range(2))
                                        mm(bank, x_hi, w_hi[:, c % RING, k], start=begin, stop=False)
                                        mm(bank, x_hi, w_lo[:, c % RING, k], start=False, stop=False)
                                        o = mm(bank, x_lo, w_hi[:, c % RING, k], start=False, stop=end)
                                    continue
                                for j in range(TG):
                                    hi, lo = (w[:, c % RING, k, j * P:(j + 1) * P] for w in (w_hi, w_lo))
                                    mm(to[:, j, :], hi, src[:, t, 0, :], start=begin and j % 2 == 0, stop=False,
                                       skip_group_check=True)
                                    mm(to[:, j, :], hi, src[:, t, 1, :], start=False, stop=False, skip_group_check=True)
                                    o = mm(to[:, j, :], lo, src[:, t, 0, :], start=False, stop=end, skip_group_check=True)
                            o.then_inc(chunk_used, 1)
                            if carry and first:
                                carry(g, kk)
                            if first and rs and (g, kk) == rs_at:
                                sum_squares(*rs)
                            if pieces:
                                pieces(i, first, g, kk)
                loop(pe, phase, body)

            pe.sem_inc(chunk_used, RING)
            pe.wait_ge(ident_loaded, 16)

            def turn_x(g):
                pe.wait_ge(x_loaded[g], 16)
                stage(S_X[g], [turn(x_tok[:, b, (g * TG + j) * P:(g * TG + j + 1) * P], j * T + b * P)
                               for j in range(TG) for b in range(T // P)])

            turn_x(0)
            pe.wait_ge(rows_loaded, 16 * 4)
            stage(S_PAR, [turn(rows[:, 0, :], 0)])
            turn_x(1)
            pe.wait_ge(inits, 3)

            def output(i, g, kk):
                if (g, kk) != (0, 2):
                    return
                pe.wait_ge(acc_free, at(i, HGRN_IN.groups, V_GROUP + 1 + SETS))
                pe.wait_ge(stage_free, at(i, HGRN_STAGES, S_HGRN + HGRN_STAGES - 1 + STAGES))
                steps = []
                for j in range(TG):
                    for b, a, col, begin, end in ((0, a_diag[:, j, 0], 0, j % 2 == 0, True),
                                                  (0, a_off[:, j], P, False, False),
                                                  (1, a_diag[:, j, 1], P, False, True)):
                        steps.append(lambda to, j=j, b=b, a=a, col=col, begin=begin, end=end: mm(
                            to[:, j * T + col:j * T + col + P], vt[:, j, b], a, start=begin, stop=end,
                            skip_group_check=True))
                stage(S_HGRN + HGRN_STAGES - 1, steps, i, HGRN_STAGES)

            def hgrn(i, first, g, kk):
                if first and g == 0 and kk in X_LATE:
                    turn_x(X_LATE[kk])
                if first and (g, kk) == (0, CONV_PAR_AT):
                    pe.wait_ge(conv_rows_loaded, 16 * 4)
                    stage(S_CONV_PAR, [turn(rows[0:4 * DT, 1, :], 0, 4 * DT)] +
                          [turn(rows[:, 2 + t, :], (1 + t) * P) for t in range(4)] +
                          [turn(rows[0:FFN_ROWS - 4 * P, 6, :], 5 * P, FFN_ROWS - 4 * P)])
                if not first:
                    output(i - 1, g, kk)
                n = g * HGRN_IN.cpg + kk - 2 * HGRN_IN.cpg
                for s, (after, what, m) in enumerate(PLAN):
                    if n != after or what == OUTPUT:
                        continue
                    if what == LEVEL:
                        lhs = kh[:] if m < 1 else kl[:, m % 2]
                        pe.wait_ge(qk_ready, at(i, 1 + len(LEVELS), m + 2))
                        if m < 0:
                            steps = [lambda to, j=j, b=b: mm(to[:, (2 * j + b) * P:(2 * j + b + 1) * P],
                                                             lhs[:, j, b * P:(b + 1) * P], qh[:, j, b * P:(b + 1) * P],
                                                             start=True, stop=True)
                                     for j in range(TG) for b in range(2)]
                        elif LEVELS[m] < P:
                            rows_s = HALF if LEVELS[m] == HALF else P
                            steps = [lambda to, j=j, b=b: mm(to[0:rows_s, (2 * j + b) * HALF:(2 * j + b + 1) * HALF],
                                                             lhs[:, j, b * P:b * P + rows_s],
                                                             ql[:, m % 2, j, b * HALF:(b + 1) * HALF],
                                                             start=True, stop=True)
                                     for j in range(TG) for b in range(2)]
                        else:
                            steps = [lambda to, j=j: mm(to[:, j * P:(j + 1) * P], lhs[:, j, 0:P], ql[:, m % 2, j, :],
                                                        start=True, stop=True) for j in range(TG)]
                    stage(S_HGRN + s, steps, i, HGRN_STAGES)

            G = DT // TG
            phase_of(HGRN_IN, xn, xn_ready, 0, (0, S_RS_HGRN, True), hgrn, rs_at=divmod(LATE_RS_AT, HGRN_IN.cpg),
                     token_group=V_GROUP)
            phase_of(HGRN_OUT, act, act_ready, 0, (1, S_RS_OUT), carry=lambda g, kk: output(HGRN_IN.n - 1, g, kk))
            phase_of(UP0, xn, xn_ready, G, (2, S_RS_UP0))
            phase_of(DOWN0, act, act_ready, G)
            phase_of(SC_IN, xn, xn_ready, 2 * G, (3, S_RS_SC))
            phase_of(SC_OUT, act, act_ready, G + UP0.n)
            phase_of(UP1, xn, xn_ready, 3 * G, (4, S_RS_UP1))

            def turn_y(n):
                pe.wait_ge(y_ready, n + 1)
                stage(S_Y + n, [turn(tb[:, j, b * P:(b + 1) * P], (b * TG + j) * P)
                                for b in range(T // P) for j in range(TG)])

            def turn_before(i, first, g, kk):
                if kk == RING and i * 2 + g:
                    turn_y(i * 2 + g - 1)

            phase_of(DOWN1, act, act_ready, 2 * G + UP0.n, pieces=turn_before)
            pe.wait_ge(y_ready, G)
            turn_y(G - 1)
            pe.wait_ge(sq_sum, G * 6)
            stage(S_RS_END, token_sums(0))


_INS = ["x", "norm_mix", "norm_ffn", "hgrn_w_in", "hgrn_lb_table", "hgrn_out_norm", "hgrn_w_out", "sc_w_in",
        "sc_conv", "sc_w_out", "ffn_w_up", "ffn_conv", "ffn_w_down", "final_norm"]


def kernel(**inputs):
    import numpy as np
    import concourse.bacc as bacc
    from concourse.bass_utils import run_bass_kernel_spmd

    nc = bacc.Bacc("TRN2", target_bir_lowering=False, num_devices=1)
    arrays = {f"in_{name}": np.ascontiguousarray(inputs[name]) for name in _INS}
    s, t = np.arange(P)[:, None], np.arange(P)[None, :]
    pairs = [((s // (2 * n) == t // (2 * n)) & (s // n % 2 == 0))[:, np.arange(P) // n % 2 == 1] for n in LEVELS[:-2]]
    arrays["in_identity"] = np.eye(P, dtype=np.float32)
    arrays["in_level_masks"] = np.concatenate([s == t] + pairs, axis=1).astype(np.float32)
    args = [nc.dram_tensor(k, a.shape, mybir.dt.from_np(a.dtype), kind="ExternalInput").ap() for k, a in arrays.items()]
    args.append(nc.dram_tensor("out", (1, T, D), F32, kind="ExternalOutput").ap())
    trunk(nc, *args)
    return run_bass_kernel_spmd(nc, [arrays], core_ids=[0]).results[0]["out"]
```
